# Optimizing a Trainium2 kernel written in Bass

```python
import jax, jax.numpy as jnp
from jax import lax
import numpy as np

D_MODEL = 2048
BATCH = 1
SEQ = 128
DEPTH = 1
DEC_BATCH = 1
DEC_SEQ = 512
PAST_LEN = 128

GRID_W = 64
N_MOD = 6
EPS = 1e-6
DN_HEADS = 8
DN_DK = 128
DN_DV = 128
DN_CHUNK = 64
CONV_K = 3
QK_W = DN_HEADS * DN_DK
V_W = DN_HEADS * DN_DV
GM_GROUPS = 8
GM_CH = 128
GM_WIDTH = GM_GROUPS * GM_CH
GM_CHUNK = 128
N_IN = 2 * QK_W + 2 * V_W + 4 * DN_HEADS + 2 * GM_WIDTH + 2 * D_MODEL
PEER_HEADS = 8
PEER_NKEYS = 128
PEER_EXPERTS = PEER_NKEYS * PEER_NKEYS
PEER_DKEY = 256
PEER_TOPK = 16
PEER_TOKEN_BLOCK = 128

kernel_name = "hybrid_deltanet_gmlp_peer_diffusion_step"

def rmsnorm(x, w):
    xf = x.astype(jnp.float32)
    y = xf * lax.rsqrt(jnp.mean(xf * xf, axis=-1, keepdims=True) + EPS)
    return (y * w.astype(jnp.float32)).astype(x.dtype)

def l2norm(x):
    xf = x.astype(jnp.float32)
    return (xf * lax.rsqrt(jnp.sum(xf * xf, axis=-1, keepdims=True) + EPS)).astype(x.dtype)

def split_last(a, sizes):
    return jnp.split(a, np.cumsum(sizes)[:-1].tolist(), axis=-1)

def grid_pos_embed(T, dtype):
    rows = T // GRID_W
    r, col = jnp.meshgrid(jnp.arange(rows, dtype=jnp.float32), jnp.arange(GRID_W, dtype=jnp.float32), indexing='ij')
    quarter = D_MODEL // 4
    freq = 1.0 / (10000.0 ** (jnp.arange(quarter, dtype=jnp.float32) / quarter))

    def enc(p):
        ang = p.reshape(-1, 1) * freq
        return jnp.concatenate([jnp.sin(ang), jnp.cos(ang)], axis=-1)

    return jnp.concatenate([enc(r), enc(col)], axis=-1).astype(dtype)

def adaln(cond, w_mod, b_mod):
    m = jax.nn.silu(cond) @ w_mod + b_mod
    return m.reshape(cond.shape[0], N_MOD, D_MODEL)

def short_conv(x, w):
    C = x.shape[-1]
    return lax.conv_general_dilated(x, w[:, None, :].astype(x.dtype), window_strides=(1,),
                                    padding=[(CONV_K // 2, CONV_K // 2)],
                                    dimension_numbers=('NWC', 'WIO', 'NWC'), feature_group_count=C)

def gated_delta_chunked(q, k, v, g, beta, s0):
    B, T, H, _ = q.shape
    n = T // DN_CHUNK
    f32 = jnp.float32

    def to_chunks(a):
        a = a.astype(f32).reshape((B, n, DN_CHUNK, H) + a.shape[3:])
        return jnp.moveaxis(a, (1, 3), (0, 2))

    qc = to_chunks(q) * (DN_DK ** -0.5)
    kc = to_chunks(k)
    vc = to_chunks(v)
    bc = to_chunks(beta)
    gc = jnp.cumsum(to_chunks(g), axis=-1)
    idx = jnp.arange(DN_CHUNK)
    causal = idx[:, None] >= idx[None, :]
    strict = idx[:, None] > idx[None, :]
    decay = jnp.exp(jnp.where(causal, gc[..., :, None] - gc[..., None, :], -jnp.inf))
    kb = kc * bc[..., None]
    m = jnp.where(strict, jnp.einsum('nbhid,nbhjd->nbhij', kb, kc) * decay, 0.0)
    tri = m + jnp.eye(DN_CHUNK, dtype=f32)
    rhs = jnp.concatenate([vc * bc[..., None], kb * jnp.exp(gc)[..., None]], axis=-1)
    sol = lax.linalg.triangular_solve(tri, rhs, left_side=True, lower=True, unit_diagonal=True)
    u_c, w_c = sol[..., :DN_DV], sol[..., DN_DV:]
    qk = jnp.einsum('nbhid,nbhjd->nbhij', qc, kc) * decay

    def step(S, xs):
        qi, ki, ui, wi, gi, qki = xs
        v_new = ui - jnp.einsum('bhcd,bhde->bhce', wi, S)
        o = (jnp.einsum('bhcd,bhde->bhce', qi * jnp.exp(gi)[..., None], S)
             + jnp.einsum('bhij,bhje->bhie', qki, v_new))
        glast = gi[..., -1]
        S = (S * jnp.exp(glast)[..., None, None]
             + jnp.einsum('bhcd,bhce->bhde', ki * jnp.exp(glast[..., None] - gi)[..., None], v_new))
        return S, o

    S, o = lax.scan(step, s0.astype(f32), (qc, kc, u_c, w_c, gc, qk))
    o = jnp.moveaxis(o, (0, 2), (1, 3)).reshape(B, T, H, DN_DV)
    return o.astype(v.dtype), S.astype(v.dtype)

def chunk_spatial_gate(u, vg, norm_w, w_s, b_s):
    B, T, _ = u.shape
    n = T // GM_CHUNK
    u = jax.nn.gelu(u)
    vg = rmsnorm(jax.nn.gelu(vg), norm_w).reshape(B, n, GM_CHUNK, GM_GROUPS, GM_CH)
    mixed = jnp.einsum('gts,bnsgc->bntgc', w_s, vg) + b_s.T[None, None, :, :, None]
    return u * mixed.reshape(B, T, GM_WIDTH)

def peer(h, w_query, sub_keys, expert_u, expert_v):
    B, T, D = h.shape
    q = jnp.einsum('btd,dhk->bthk', h, w_query).reshape(B, T, PEER_HEADS, 2, PEER_DKEY // 2)
    s = jnp.einsum('bthpk,hpnk->bthpn', q, sub_keys)
    sv, si = lax.top_k(s, PEER_TOPK)
    cand = (sv[..., 0, :, None] + sv[..., 1, None, :]).reshape(B, T, PEER_HEADS, PEER_TOPK * PEER_TOPK)
    cidx = (si[..., 0, :, None] * PEER_NKEYS + si[..., 1, None, :]).reshape(B, T, PEER_HEADS, PEER_TOPK * PEER_TOPK)
    best, pos = lax.top_k(cand, PEER_TOPK)
    eidx = jnp.take_along_axis(cidx, pos, axis=-1)
    gates = jax.nn.softmax(best.astype(jnp.float32), axis=-1).astype(h.dtype)
    nb = (B * T) // PEER_TOKEN_BLOCK
    hb = h.reshape(nb, PEER_TOKEN_BLOCK, D)
    ib = eidx.reshape(nb, PEER_TOKEN_BLOCK, PEER_HEADS * PEER_TOPK)
    gb = gates.reshape(nb, PEER_TOKEN_BLOCK, PEER_HEADS * PEER_TOPK)

    def block(args):
        hx, ix, gx = args
        act = jax.nn.gelu(jnp.einsum('nd,ned->ne', hx, expert_u[ix]))
        return jnp.einsum('ne,ned->nd', act * gx, expert_v[ix])

    return lax.map(block, (hb, ib, gb)).reshape(B, T, D)

def trunk_layer(x, mod, s0, lp):
    B, T, _ = x.shape
    sh1, sc1, gt1, sh2, sc2, gt2 = [mod[:, i, None, :] for i in range(N_MOD)]
    h = rmsnorm(x, lp['norm_mix']) * (1 + sc1) + sh1
    proj = h @ lp['w_in']
    qkv, z, bf, bb, af, ab, u, vg, ga, gb = split_last(
        proj, [2 * QK_W + V_W, V_W, DN_HEADS, DN_HEADS, DN_HEADS, DN_HEADS, GM_WIDTH, GM_WIDTH, D_MODEL, D_MODEL])
    qkv = jax.nn.silu(short_conv(qkv, lp['conv_w']))
    q, k, v = split_last(qkv, [QK_W, QK_W, V_W])
    q = l2norm(q.reshape(B, T, DN_HEADS, DN_DK))
    k = l2norm(k.reshape(B, T, DN_HEADS, DN_DK))
    v = v.reshape(B, T, DN_HEADS, DN_DV)
    beta = jax.nn.sigmoid(jnp.stack([bf, bb], 0).astype(jnp.float32))
    a = jnp.stack([af, ab], 0).astype(jnp.float32)
    g = (-jnp.exp(lp['dn_a_log'].astype(jnp.float32))[:, None, None, :]
         * jax.nn.softplus(a + lp['dn_dt_bias'].astype(jnp.float32)[:, None, None, :]))
    o_f, s_f = gated_delta_chunked(q, k, v, g[0], beta[0], s0[:, 0])
    flip = lambda t: jnp.flip(t, axis=1)
    o_b, s_b = gated_delta_chunked(flip(q), flip(k), flip(v), flip(g[1]), flip(beta[1]), s0[:, 1])
    o = o_f + flip(o_b)
    o = rmsnorm(o, lp['dn_norm']) * jax.nn.silu(z.reshape(B, T, DN_HEADS, DN_DV))
    p_a = o.reshape(B, T, V_W) @ lp['w_branch_a']
    p_b = chunk_spatial_gate(u, vg, lp['gm_norm'], lp['gm_w_s'], lp['gm_b_s']) @ lp['w_branch_b']
    merged = jax.nn.sigmoid(ga) * p_a + jax.nn.sigmoid(gb) * p_b
    x = x + gt1 * (merged @ lp['w_out'])
    h2 = rmsnorm(x, lp['norm_ffn']) * (1 + sc2) + sh2
    x = x + gt2 * peer(h2, lp['peer_w_query'], lp['peer_sub_keys'], lp['peer_u'], lp['peer_v'])
    return x, jnp.stack([s_f, s_b], axis=1)

def setup_inputs(seed: int = 0) -> dict:
    key = jax.random.key(seed)
    ks = jax.random.split(key, 32)
    f32 = jnp.float32
    L, D = DEPTH, D_MODEL
    nrm = lambda k, shape, scale: jax.random.normal(k, shape, f32) * scale
    dt = jnp.exp(jax.random.uniform(ks[11], (L, 2, DN_HEADS), f32, np.log(1e-3), np.log(1e-1)))
    return {
        'x_prompt': nrm(ks[0], (BATCH, SEQ, D), 1.0),
        'x_sample': nrm(ks[1], (DEC_BATCH, DEC_SEQ, D), 1.0),
        'state_delta': nrm(ks[2], (DEC_BATCH, DEPTH, 2, DN_HEADS, DN_DK, DN_DV), DN_DK ** -0.5),
        'c': nrm(ks[3], (DEC_BATCH, D), 1.0),
        'c_ctx': nrm(ks[4], (D,), 1.0),
        'w_mod': nrm(ks[5], (L, D, N_MOD * D), D ** -0.5),
        'b_mod': nrm(ks[6], (L, N_MOD * D), 0.02),
        'norm_mix': 1.0 + nrm(ks[7], (L, D), 0.02),
        'w_in': nrm(ks[8], (L, D, N_IN), D ** -0.5),
        'conv_w': nrm(ks[9], (L, CONV_K, 2 * QK_W + V_W), CONV_K ** -0.5),
        'dn_a_log': jnp.log(jax.random.uniform(ks[10], (L, 2, DN_HEADS), f32, 1.0, 16.0)),
        'dn_dt_bias': dt + jnp.log(-jnp.expm1(-dt)),
        'dn_norm': 1.0 + nrm(ks[12], (L, DN_DV), 0.02),
        'gm_norm': 1.0 + nrm(ks[13], (L, GM_WIDTH), 0.02),
        'gm_w_s': nrm(ks[14], (L, GM_GROUPS, GM_CHUNK, GM_CHUNK), GM_CHUNK ** -0.5),
        'gm_b_s': 1.0 + nrm(ks[15], (L, GM_GROUPS, GM_CHUNK), 0.02),
        'w_branch_a': nrm(ks[16], (L, V_W, D), V_W ** -0.5),
        'w_branch_b': nrm(ks[17], (L, GM_WIDTH, D), GM_WIDTH ** -0.5),
        'w_out': nrm(ks[18], (L, D, D), D ** -0.5),
        'norm_ffn': 1.0 + nrm(ks[19], (L, D), 0.02),
        'peer_w_query': nrm(ks[20], (L, D, PEER_HEADS, PEER_DKEY), D ** -0.5),
        'peer_sub_keys': nrm(ks[21], (L, PEER_HEADS, 2, PEER_NKEYS, PEER_DKEY // 2), (PEER_DKEY // 2) ** -0.5),
        'peer_u': nrm(ks[22], (L, PEER_EXPERTS, D), D ** -0.5),
        'peer_v': nrm(ks[23], (L, PEER_EXPERTS, D), PEER_HEADS ** -0.5),
        'norm_final': 1.0 + nrm(ks[24], (D,), 0.02),
    }

def reference(x_prompt, x_sample, state_delta, c, c_ctx, w_mod, b_mod, norm_mix, w_in, conv_w,
              dn_a_log, dn_dt_bias, dn_norm, gm_norm, gm_w_s, gm_b_s, w_branch_a, w_branch_b, w_out,
              norm_ffn, peer_w_query, peer_sub_keys, peer_u, peer_v, norm_final):
    xp = x_prompt
    xs = x_sample + grid_pos_embed(x_sample.shape[1], x_sample.dtype)[None]
    ctx_s0 = jnp.zeros((x_prompt.shape[0], 2, DN_HEADS, DN_DK, DN_DV), x_prompt.dtype)
    new_states = []
    for l in range(DEPTH):
        lp = {
            'norm_mix': norm_mix[l], 'w_in': w_in[l], 'conv_w': conv_w[l], 'dn_a_log': dn_a_log[l],
            'dn_dt_bias': dn_dt_bias[l], 'dn_norm': dn_norm[l], 'gm_norm': gm_norm[l], 'gm_w_s': gm_w_s[l],
            'gm_b_s': gm_b_s[l], 'w_branch_a': w_branch_a[l], 'w_branch_b': w_branch_b[l], 'w_out': w_out[l],
            'norm_ffn': norm_ffn[l], 'peer_w_query': peer_w_query[l], 'peer_sub_keys': peer_sub_keys[l],
            'peer_u': peer_u[l], 'peer_v': peer_v[l],
        }
        mod_ctx = adaln(c_ctx[None, :], w_mod[l], b_mod[l])
        mod_lat = adaln(c, w_mod[l], b_mod[l])
        xp, st = trunk_layer(xp, mod_ctx, ctx_s0, lp)
        new_states.append(st)
        xs, _ = trunk_layer(xs, mod_lat, state_delta[:, l], lp)
    y_prompt = rmsnorm(xp, norm_final)
    y_sample = rmsnorm(xs, norm_final)
    new_state_delta = jnp.stack(new_states, axis=1)
    return (y_prompt, y_sample, new_state_delta)


_drawn_inputs = setup_inputs


def setup_inputs(seed=0):
    import zlib

    import numpy as np

    out = dict(_drawn_inputs(seed))
    spreads = {}
    factors = {'dn_norm': 22.505,
     'gm_norm': 20.016,
     'gm_b_s': 22.832,
     'norm_ffn': 10.89,
     'norm_final': 8.146}
    for name, (base, spread) in spreads.items():
        noise = np.random.default_rng([zlib.crc32(name.encode()), seed]).standard_normal(out[name].shape)
        drawn = base * np.exp(spread * noise) if base else spread * noise
        out[name] = __import__('jax').numpy.asarray(drawn.astype(out[name].dtype))
    for name, factor in factors.items():
        out[name] = (out[name] * factor).astype(out[name].dtype)
    return out
```

```python
from contextlib import ExitStack

import numpy as np

import concourse.bass as bass
from concourse import mybir
from concourse.alu_op_type import AluOpType as ALU

ACT = mybir.ActivationFunctionType
AX_X = mybir.AxisListType.X
F32 = mybir.dt.float32
I32 = mybir.dt.int32
U32 = mybir.dt.uint32

P = 128
D = 2048
KD = D // P
NB = 5
NT = NB * P
LAT = NT - P
H = 8
HD = H * P
NMOD = 6
TOPK = 16
NKEYS = 128
EPS = 1e-6
COL = 512
RING = 6
TILE = 2048
LEVELS = 7
BIG = 1e30
LOWEST = -3.0e38
SH1, SC1, GT1, SH2, SC2, GT2 = range(NMOD)


class Store:
    pass


class Chain:

    def __init__(self, engine, sem):
        self.engine, self.sem, self.base, self.count = engine, sem, 0, 0

    def sig(self, instruction):
        instruction.then_inc(self.sem, 1)
        self.count += 1

    def sync(self):
        self.engine.wait_ge(self.sem, self.base + self.count)

    def step(self, instruction):
        self.sig(instruction)
        self.sync()

    def enter(self, i, per):
        self.outer = (self.base + self.count, per)
        self.base, self.count = self.outer[0] + i * per, 0

    def leave(self, passes):
        before, per = self.outer
        assert self.count == per, (self.count, per)
        self.base, self.count = before + passes * per, 0


def col(ap, i):
    return ap[:, bass.ds(i, 1)]


def wide(ap, n):
    return ap.unsqueeze(2).to_broadcast([P, ap.shape[1], n])


def over(ap, n):
    return ap.unsqueeze(1).to_broadcast([P, n, ap.shape[1]])



def allocate(nc, ctx):
    def sb(name, shape, dtype=F32):
        return ctx.enter_context(nc.sbuf_tensor(f"{name}_sb", [P, *shape], dtype))

    t = Store()
    t.ring = sb("ring", [4, TILE])
    t.hx = sb("hx", [KD * NT])
    t.c = sb("c_region", [3 * H * NT])
    t.d = sb("d_region", [12288])
    t.e = sb("e_region", [4096])
    t.ident = sb("ident", [P])
    t.tri = sb("tri", [2, P])
    t.ones = sb("ones", [P])
    t.small = sb("small", [64])
    t.cw = sb("cw", [3 * H, 3])
    t.cond = sb("cond", [KD, 2])
    t.scond = sb("scond", [KD, 2])
    t.scale1 = sb("scale1", [KD, 2])
    t.shift1 = sb("shift1", [KD, 2])
    t.beta = sb("beta", [NB, 2 * H])
    t.log_decay = sb("log_decay", [NB, 2 * H])
    t.beg = sb("beg", [NB, 2 * H])
    t.g = sb("g", [NB, 2 * H])
    t.stat = sb("stat", [64])
    t.place = sb("place", [3, TOPK], U32)
    t.index = sb("index", [2, TOPK], I32)
    t.ps = ctx.enter_context(nc.psum_tensor("ps", [P, 8, COL], F32))
    t.mod_rows = nc.dram_tensor("mod_rows", (2, NMOD * D), F32).ap()
    t.sem = lambda name: ctx.enter_context(nc.semaphore(name))
    t.full = [t.sem(f"ring_full{s}") for s in range(4)]
    t.tile_done = t.sem("tile_done")
    t.x_in, t.init, t.passed = t.sem("x_in"), t.sem("init"), t.sem("passed")
    t.tiles = 0
    t.eps, t.iota, t.qk_scale, t.dn_norm = t.small[:, 0:1], t.small[:, 1:17], t.small[:, 17:33], t.small[:, 33:34]
    return t


def tile_full(e, t, slot, use):
    e.wait_ge(t.full[slot], 16 * (t.tiles // 4 + use + 1))


def done_count(t, g):
    return t.tiles + g + 5


def load_tile(e, t, src, g, slot, tile):
    e.wait_ge(t.tile_done, t.tiles + g + 1)
    e.dma_start(t.ring[:, slot, 0:src.shape[2]],
                src[bass.ds(tile, 1)].rearrange("a p n -> (a p) n")).then_inc(t.full[slot], 16)


def stream(e, t, src, tiles):
    with e.Fori(0, tiles // 4) as i:
        for s in range(4):
            load_tile(e, t, src, 4 * i + s, s, 4 * i + s)



def modulation(nc, t, a):
    w_tiles = NMOD * D // COL * 4
    cond_in, bias_in, silu_done = t.sem("cond_in"), t.sem("bias_in"), t.sem("silu_done")
    bank_free, row_out, turned = t.sem("mod_bank_free"), t.sem("mod_row_out"), t.sem("mod_turned")
    rows = t.c[0:2, KD * NT:KD * NT + 10 * COL]
    bias = t.d[0:2, :]
    with nc.Block() as block:
        @block.sync
        def _(sp):
            sp.dma_start(t.cond[:], a["cond"]).then_inc(cond_in, 16)
            sp.dma_start(t.ident[:], a["c_ident"]).then_inc(cond_in, 16)
            sp.dma_start(bias, a["b_mod"].partition_broadcast(2)).then_inc(bias_in, 16)
            stream(sp, t, a["w_mod"], w_tiles)

        @block.scalar
        def _(act):
            for b in range(NB):
                act.dma_start(t.c[:, b * D:(b + 1) * D], a["x"][b]).then_inc(t.x_in, 16)
            act.dma_start(t.tri[:], a["c_tri"]).then_inc(t.x_in, 16)
            act.dma_start(t.small[:, 1:33], a["c_small"]).then_inc(t.x_in, 16)
            act.dma_start(t.small[:, 33:34], a["dn_norm"]).then_inc(t.x_in, 16)
            act.dma_start(t.cw[:], a["conv_w"]).then_inc(t.x_in, 16)
            act.dma_start(t.stat[:, 0:16], a["a_log"].partition_broadcast(P)).then_inc(t.x_in, 16)
            act.dma_start(t.stat[:, 16:32], a["dt_bias"].partition_broadcast(P)).then_inc(t.x_in, 16)
            act.dma_start(t.stat[:, 32:48], a["norm_mix"]).then_inc(t.x_in, 16)
            act.wait_ge(cond_in, 32)
            nc.scalar.activation(t.scond[:], t.cond[:], ACT.Silu).then_inc(silu_done, 1)
            act.sem_inc(row_out, 32)
            with act.Fori(4, 12) as i:
                for q in range(2):
                    act.wait_ge(bank_free, 2 * i + q + 3)
                    act.dma_start(t.mod_rows[:, bass.ds((2 * i + q) * COL, COL)],
                                  rows[:, (8 + q) * COL:(9 + q) * COL]).then_inc(row_out, 16)
                    act.wait_ge(row_out, 32 + 16 * (2 * i + q - 7))

        @block.tensor
        def _(pe):
            pe.sem_inc(t.tile_done, 4)
            pe.wait_ge(silu_done, 1)
            with pe.Fori(0, 12) as i:
                for q in range(2):
                    pe.wait_ge(bank_free, 2 * i + q + 1)
                    for kq in range(4):
                        tile_full(pe, t, kq, 2 * i + q)
                        for kk in range(4):
                            k = 4 * kq + kk
                            mm = pe.matmul(t.ps[0:2, q, :], t.scond[:, k, :],
                                           t.ring[:, kq, kk * COL:(kk + 1) * COL],
                                           start=(k == 0), stop=(k == KD - 1))
                        mm.then_inc(t.tile_done, 1)
            pe.wait_ge(bank_free, 10)
            for j in range(2 * KD):
                mm = pe.transpose(t.ps[:, 2, 2 * j:2 * j + 2], rows[:, j * P:(j + 1) * P],
                                  t.ident[0:2, 0:2])
            mm.then_inc(turned, 1)

        @block.vector
        def _(dve):
            nc.vector.memset(t.ones[:], 1.0).then_inc(t.init, 1)
            nc.vector.memset(t.eps, EPS).then_inc(t.init, 1)
            dve.sem_inc(bank_free, 2)
            dve.wait_ge(bias_in, 16)
            for first, last in ((0, 4), (4, 12)):
                with dve.Fori(first, last) as i:
                    for q in range(2):
                        n = 2 * i + q
                        if first:
                            dve.wait_ge(row_out, 16 * (n - 7))
                            out = rows[:, (8 + q) * COL:(9 + q) * COL]
                        else:
                            out = rows[:, bass.ds(n * COL, COL)]
                        dve.wait_ge(t.tile_done, done_count(t, 4 * n + 3))
                        nc.vector.tensor_tensor(out, t.ps[0:2, q, :], bias[:, bass.ds(n * COL, COL)],
                                                ALU.add).then_inc(bank_free, 1)
            dve.wait_ge(turned, 1)
            dve.wait_ge(t.x_in, 16 * 12)
            nc.vector.tensor_copy(t.shift1[:].rearrange("p k c -> p (k c)"),
                                  t.ps[:, 2, 0:2 * KD]).then_inc(t.init, 1)
            nc.vector.scalar_tensor_tensor(
                out=t.scale1[:], in0=t.ps[:, 2, 2 * KD:4 * KD].rearrange("p (k c) -> p k c", c=2),
                scalar=1.0, in1=wide(t.stat[:, 32:48], 2), op0=ALU.add, op1=ALU.mult).then_inc(t.init, 1)
    t.tiles += w_tiles



def mixer_input(nc, t, a):
    pos_in, x_done, sumsq, rstd = t.sem("pos_in"), t.sem("x_done"), t.sem("sumsq1"), t.sem("rstd1")
    xn_done, turned = t.sem("xn_done"), t.sem("xn_turned")
    lat_read, ctx_read = t.sem("lat_bank_read1"), t.sem("ctx_bank_read1")
    ss, root, inv = t.stat[:, 48:53], t.stat[:, 53:58], t.stat[:, 58:63]
    with nc.Block() as block:
        @block.sync
        def _(sp):
            for b in range(1, NB):
                sp.dma_start(t.d[:, (b - 1) * D:b * D], a["c_pos"][b - 1]).then_inc(pos_in, 16)

        @block.vector
        def _(dve):
            dve.wait_ge(pos_in, 64)
            for b in range(1, NB):
                x = t.c[:, b * D:(b + 1) * D]
                nc.vector.tensor_tensor(x, x, t.d[:, (b - 1) * D:b * D], ALU.add).then_inc(x_done, 1)
            dve.wait_ge(sumsq, NB)
            nc.vector.tensor_scalar(root, ss, 1.0 / D, EPS, ALU.mult, ALU.add).then_inc(rstd, 1)
            dve.wait_ge(rstd, 2)
            nc.vector.reciprocal(inv, root).then_inc(rstd, 1)
            dve.wait_ge(rstd, 3)
            for b in range(NB):
                x = t.c[:, b * D:(b + 1) * D]
                nc.vector.tensor_scalar(x, x, inv[:, b:b + 1], None, ALU.mult).then_inc(xn_done, 1)
            dve.sem_inc(lat_read, 2)
            for k in range(KD):
                dve.wait_ge(turned, k + 1)
                nc.vector.tensor_scalar(t.hx[:, k * NT + P:(k + 1) * NT], t.ps[:, 2 * (k % 2), :],
                                        t.scale1[:, k, 1:2], t.shift1[:, k, 1:2],
                                        ALU.mult, ALU.add).then_inc(lat_read, 1)

        @block.scalar
        def _(act):
            for b in range(NB):
                if b:
                    act.wait_ge(x_done, b)
                nc.scalar.activation(t.ps[:, 4:8, :].rearrange("p a n -> p (a n)"), t.c[:, b * D:(b + 1) * D],
                                     ACT.Square, accum_out=ss[:, b:b + 1]).then_inc(sumsq, 1)
                act.wait_ge(sumsq, b + 1)
            act.wait_ge(rstd, 1)
            nc.scalar.activation(root, root, ACT.Sqrt).then_inc(rstd, 1)
            act.sem_inc(ctx_read, 2)
            for k in range(KD):
                act.wait_ge(turned, k + 1)
                nc.scalar.activation(t.hx[:, k * NT:k * NT + P], t.ps[:, 2 * (k % 2) + 1, 0:P], ACT.Identity,
                                     bias=t.shift1[:, k, 0:1], scale=t.scale1[:, k, 0:1]).then_inc(ctx_read, 1)

        @block.tensor
        def _(pe):
            pe.wait_ge(xn_done, NB)
            for k in range(KD):
                pe.wait_ge(lat_read, k + 1)
                pe.wait_ge(ctx_read, k + 1)
                for b in range(NB):
                    out = t.ps[:, 2 * (k % 2), (b - 1) * P:b * P] if b else t.ps[:, 2 * (k % 2) + 1, 0:P]
                    mm = pe.transpose(out, t.c[:, b * D + k * P:b * D + (k + 1) * P], t.ident[:])
                mm.then_inc(turned, 1)



def project(pe, t, pair, weights, x, chunks=KD):
    for k in range(chunks):
        w = weights[:, k * P:(k + 1) * P]
        pe.matmul(t.ps[:, 2 * pair + 1, 0:P], w, x[:, k, 0:P], start=(k == 0), stop=(k == chunks - 1))
        mm = pe.matmul(t.ps[:, 2 * pair, :], w, x[:, k, P:NT], start=(k == 0), stop=(k == chunks - 1))
    return mm


def qkv(nc, t, a):
    h = t.hx[:].rearrange("p (k n) -> p k n", k=KD)
    y = [t.d[:, i * NT:(i + 1) * NT] for i in range(2)]
    s = [t.d[:, (2 + i) * NT:(3 + i) * NT] for i in range(2)]
    sq, norm = t.d[:, 4 * NT:5 * NT], t.d[:, 5 * NT:6 * NT]
    wg = t.d[:, 6 * NT:6 * NT + KD * 32].rearrange("p (k n) -> p k n", k=KD)
    consts_in = t.sem("gate_w_in")
    conv_step, psum_read = t.sem("conv_step"), t.sem("conv_psum_read")
    silu_done, sq_done, norm_ps, norm_step, qk_done = (t.sem(n) for n in (
        "qkv_silu", "qk_square", "qk_norm_sum", "qk_norm_step", "qk_done"))
    gates_ps, gates, cum_ps = t.sem("gates_psum"), t.sem("gates_step"), t.sem("cumsum_psum")
    tiles, with_norm = 3 * H, 2 * H

    with nc.Block() as block:
        @block.sync
        def _(sp):
            sp.dma_start(wg, a["w_gates"]).then_inc(consts_in, 16)
            sp.dma_start(t.d[:, 5120:5120 + 2304], a["c_masks"]).then_inc(consts_in, 16)
            stream(sp, t, a["w_qkv"], tiles)

        @block.tensor
        def _(pe):
            def norm_sum(n):
                pe.wait_ge(sq_done, n + 1)
                pe.matmul(t.ps[:, 5, 0:P], t.ones[:], sq[:, 0:P], start=True, stop=True)
                pe.matmul(t.ps[:, 4, :], t.ones[:], sq[:, P:NT], start=True, stop=True).then_inc(norm_ps, 1)

            def four(i, norms):
                for j in range(4):
                    n = 4 * i + j
                    pe.wait_ge(psum_read, n + 1)
                    tile_full(pe, t, j, i)
                    project(pe, t, j % 2, t.ring[:, j, :], h).then_inc(t.tile_done, 1)
                    if j in norms:
                        norm_sum(n - 1)

            four(0, (1, 2, 3))
            with pe.Fori(1, with_norm // 4) as i:
                four(i, (0, 1, 2, 3))
            four(with_norm // 4, (0,))
            four(with_norm // 4 + 1, ())
            pe.wait_ge(consts_in, 32)
            pe.wait_ge(psum_read, tiles + 2)
            for b in range(NB):
                for k in range(KD):
                    mm = pe.matmul(t.ps[:, 6, 32 * b:32 * b + 32], h[:, k, b * P:(b + 1) * P], wg[:, k, :],
                                   start=(k == 0), stop=(k == KD - 1))
            mm.then_inc(gates_ps, 1)
            pe.wait_ge(gates, 7)
            for b in range(NB):
                for r in range(2):
                    o = 16 * b + 8 * r
                    mm = pe.matmul(t.ps[:, 7, o:o + 8], t.tri[:, r, :], t.g[:, b, 8 * r:8 * r + 8],
                                   start=True, stop=True)
            mm.then_inc(cum_ps, 1)

        @block.vector
        def _(dve):
            chain = Chain(dve, conv_step)
            dve.sem_inc(psum_read, 2)

            def conv(n, j):
                out, pair = y[j], j
                w = [t.cw[:, bass.ds(n, 1), k:k + 1].rearrange("p a b -> p (a b)") for k in range(3)]
                seqs = ((t.ps[:, 2 * pair, :], out[:, P:NT]), (t.ps[:, 2 * pair + 1, 0:P], out[:, 0:P]))
                dve.wait_ge(t.tile_done, done_count(t, n))
                dve.wait_ge(silu_done, n + 1)
                for x, o in seqs:
                    chain.sig(nc.vector.tensor_scalar(o, x, w[1], None, ALU.mult))
                chain.sync()
                for x, o in seqs:
                    m = o.shape[1]
                    chain.sig(nc.vector.scalar_tensor_tensor(out=o[:, 1:m], in0=x[:, 0:m - 1], scalar=w[0],
                                                             in1=o[:, 1:m], op0=ALU.mult, op1=ALU.add))
                chain.sync()
                (x, o), (xc, oc) = seqs
                chain.sig(nc.vector.scalar_tensor_tensor(out=o[:, 0:LAT - 1], in0=x[:, 1:LAT], scalar=w[2],
                                                         in1=o[:, 0:LAT - 1], op0=ALU.mult, op1=ALU.add))
                nc.vector.scalar_tensor_tensor(out=oc[:, 0:P - 1], in0=xc[:, 1:P], scalar=w[2],
                                               in1=oc[:, 0:P - 1], op0=ALU.mult,
                                               op1=ALU.add).then_inc(psum_read, 1)

            def normalise(n, j):
                dve.wait_ge(norm_step, 2 * n + 1)
                nc.vector.reciprocal(norm, norm).then_inc(norm_step, 1)
                dve.wait_ge(norm_step, 2 * n + 2)
                nc.vector.scalar_tensor_tensor(out=t.c[:, bass.ds(n * NT, NT)], in0=s[j],
                                               scalar=col(t.qk_scale, n), in1=norm,
                                               op0=ALU.mult, op1=ALU.mult).then_inc(qk_done, 1)

            with dve.Fori(0, with_norm // 2) as i:
                chain.enter(i, 10)
                for j in range(2):
                    conv(2 * i + j, j)
                    normalise(2 * i + j, j)
                chain.leave(with_norm // 2)
            with dve.Fori(with_norm // 2, tiles // 2) as i:
                chain.enter(i - with_norm // 2, 10)
                for j in range(2):
                    conv(2 * i + j, j)
                chain.leave((tiles - with_norm) // 2)

            raw = t.ps[:, 6, 0:32 * NB].rearrange("p (b n) -> p b n", b=NB)
            ab, soft = t.beg[:], t.log_decay[:]
            dve.wait_ge(gates_ps, 1)
            nc.vector.tensor_tensor(ab, raw[:, :, 16:32], over(t.stat[:, 16:32], NB), ALU.add).then_inc(gates, 1)
            dve.wait_ge(gates, 4)
            nc.vector.scalar_tensor_tensor(out=soft, in0=ab, scalar=0.0, in1=soft, op0=ALU.max,
                                           op1=ALU.add).then_inc(gates, 1)
            dve.wait_ge(gates, 6)
            nc.vector.scalar_tensor_tensor(out=t.g[:], in0=soft, scalar=-1.0, in1=over(t.stat[:, 0:16], NB),
                                           op0=ALU.mult, op1=ALU.mult).then_inc(gates, 1)
            dve.wait_ge(cum_ps, 1)
            nc.vector.tensor_copy(t.log_decay[:].rearrange("p a b -> p (a b)"), t.ps[:, 7, 0:80]).then_inc(gates, 1)
            dve.wait_ge(gates, 9)
            nc.vector.tensor_tensor(t.beg[:], t.beg[:], t.beta[:], ALU.mult).then_inc(gates, 1)

        @block.scalar
        def _(act):
            act.sem_inc(silu_done, 2)
            act.sem_inc(qk_done, 2)
            with act.Fori(0, with_norm // 2) as i:
                for j in range(2):
                    n = 2 * i + j
                    act.wait_ge(psum_read, n + 3)
                    act.wait_ge(conv_step, 5 * n + 5)
                    act.wait_ge(qk_done, n + 1)
                    nc.scalar.activation(s[j], y[j], ACT.Silu).then_inc(silu_done, 1)
                    act.wait_ge(silu_done, n + 3)
                    act.wait_ge(qk_done, n + 2)
                    nc.scalar.activation(sq, s[j], ACT.Square).then_inc(sq_done, 1)
                    act.wait_ge(norm_ps, n + 1)
                    nc.scalar.activation(norm[:, P:NT], t.ps[:, 4, :], ACT.Sqrt, bias=t.eps)
                    nc.scalar.activation(norm[:, 0:P], t.ps[:, 5, 0:P], ACT.Sqrt, bias=t.eps).then_inc(norm_step, 1)
            with act.Fori(with_norm // 2, tiles // 2) as i:
                for j in range(2):
                    n = 2 * i + j
                    act.wait_ge(psum_read, n + 3)
                    act.wait_ge(conv_step, 5 * n + 5)
                    nc.scalar.activation(t.c[:, bass.ds(n * NT, NT)], y[j], ACT.Silu).then_inc(silu_done, 1)
            raw = t.ps[:, 6, 0:32 * NB].rearrange("p (b n) -> p b n", b=NB)
            ab, soft = t.beg[:], t.log_decay[:]
            act.wait_ge(gates, 1)
            nc.scalar.activation(soft, ab, ACT.Abs).then_inc(gates, 1)
            act.wait_ge(gates, 2)
            nc.scalar.activation(soft, soft, ACT.Exp, scale=-1.0).then_inc(gates, 1)
            act.wait_ge(gates, 3)
            nc.scalar.activation(soft, soft, ACT.Ln, bias=1.0).then_inc(gates, 1)
            act.wait_ge(gates, 5)
            nc.scalar.activation(t.stat[:, 0:16], t.stat[:, 0:16], ACT.Exp).then_inc(gates, 1)
            nc.scalar.activation(t.beta[:], raw[:, :, 0:16], ACT.Sigmoid)
            act.wait_ge(gates, 8)
            nc.scalar.activation(t.beg[:], t.log_decay[:], ACT.Exp).then_inc(gates, 1)
    t.tiles += tiles



def deltanet(nc, t, a):
    r8 = t.ring[:].rearrange("p s (u h n) -> p (s u) h n", u=2, h=H)
    x_, xt, pm, m_, mt, lev, kbe = (r8[:, i] for i in (0, 1, 2, 3, 4, slice(5, 7), 7))
    e8 = t.e[:].rearrange("p (u h n) -> p u h n", u=4, h=H)
    kd, vn, qd, qk = (e8[:, i] for i in range(4))
    wt, gb = m_, pm
    o_all = t.d[:, 0:NB * HD].rearrange("p (b h n) -> p b h n", b=NB, h=H)
    nmask = t.d[:, 5120:6912].rearrange("p (r l n) -> p r l n", r=2, l=LEVELS)
    above = t.d[:, 6912:7168].rearrange("p (r n) -> p r n", r=2)
    below = t.d[:, 7168:7424].rearrange("p (r n) -> p r n", r=2)
    st, st2, ks, vs = (t.d[:, o:o + HD].rearrange("p (h n) -> p h n", h=H) for o in (7424, 8448, 9472, 10496))
    heads = t.c[:].rearrange("p (w n) -> p w n", n=NT)
    tail = t.stat[:, 0:8]

    def bank(i):
        return t.ps[:, i, :].rearrange("p (h n) -> p h n", h=4)

    def banks(i):
        return t.ps[:, i:i + 2, :].rearrange("p u (h n) -> p (u h) n", h=4)

    def half(ap, u):
        return ap[:, 4 * u:4 * u + 4]

    s = {n: t.sem("dn_" + n) for n in (
        "decay_ps", "gram_ps", "kq_ps", "ktok_ps", "vtok_ps", "mt_ps", "p_ps", "q_ps", "w_ps", "vn_ps",
        "o_ps", "s_ps",
        "staged", "state_scaled", "qd_done", "level_masked",
        "diff_done", "m_done", "tok_done", "x_done", "x_step", "batch_done",
        "er_done", "exp_done", "mt_copied", "p_copied", "w_copied", "vn_copied",
        "state_out", "state_in")}

    def each_batch(engine, body):
        for r in range(2):
            body(r, 0, 5 * r, True)
            with engine.Fori(0, NB - 1) as j:
                body(r, j + 1 if r == 0 else j * -1 + (NB - 1), 5 * r + 1 + j, False)

    def tokens(ap, b):
        return ap[:, :, bass.ds(b * P, P)]

    with nc.Block() as block:
        @block.sync
        def _(sp):
            for r in range(2):
                sp.wait_ge(s["batch_done"], 5 * r + 2)
                sp.dma_start(a["new_state"][r].rearrange("h d e -> d h e"), st).then_inc(s["state_out"], 16)
                sp.wait_ge(s["state_out"], 16 * (r + 1))
                sp.dma_start(st, a["state"][r].rearrange("h d e -> d h e")).then_inc(s["state_in"], 16)

        @block.gpsimd
        def _(pool):
            def batch(r, b, n, first):
                last = P - 1 if r == 0 else 0
                pool.wait_ge(s["batch_done"], n + 1)
                nc.gpsimd.tensor_copy(gb, t.g[:, b, 8 * r:8 * r + 8].unsqueeze(2).to_broadcast([P, H, P]))
                nc.gpsimd.tensor_copy(ks, tokens(heads[:, 8:16], b))
                nc.gpsimd.tensor_copy(vs, tokens(heads[:, 16:24], b)).then_inc(s["staged"], 1)
                if first:
                    nc.gpsimd.memset(st, 0.0).then_inc(s["state_scaled"], 1)
                    pool.wait_ge(s["state_scaled"], 2 * n + 1)
                else:
                    pool.wait_ge(s["state_in"], 16 * (r + 1))
                    pool.sem_inc(s["state_scaled"], 1)
                pool.wait_ge(s["er_done"], n + 1)
                nc.gpsimd.tensor_tensor(st2, st, qd[:, :, last:last + 1].to_broadcast([P, H, P]),
                                        ALU.mult).then_inc(s["state_scaled"], 1)
                pool.wait_ge(s["state_scaled"], 2 * n + 2)
                nc.gpsimd.tensor_tensor(qd, qd, tokens(heads[:, 0:8], b), ALU.mult).then_inc(s["qd_done"], 1)
                pool.wait_ge(s["mt_copied"], 2 * n + 2)
                for k in range(1, LEVELS):
                    if k >= 3:
                        pool.wait_ge(s["p_ps"], 12 * n + 2 * (k - 2))
                    nc.gpsimd.tensor_tensor(lev[:, k % 2], mt, over(nmask[:, 1 - r, k], H),
                                            ALU.mult).then_inc(s["level_masked"], 1)
            each_batch(pool, batch)

        @block.tensor
        def _(pe):
            def products(out, lhs, rhs):
                for h in range(H):
                    mm = pe.matmul(bank(out + h // 4)[:, h % 4], lhs[:, h], rhs(h), start=True, stop=True)
                return mm

            def half_products(out, u, lhs, rhs):
                for h in range(4 * u, 4 * u + 4):
                    mm = pe.matmul(bank(out + u)[:, h % 4], lhs[:, h], rhs[:, h], start=True, stop=True)
                return mm

            def batch(r, b, n, first):
                pe.wait_ge(s["staged"], n + 1)
                products(0, gb, lambda h: t.tri[:, r, :]).then_inc(s["decay_ps"], 1)
                products(2, ks, lambda h: ks[:, h]).then_inc(s["gram_ps"], 1)
                q = tokens(heads[:, 0:8], b)
                products(4, ks, lambda h: q[:, h]).then_inc(s["kq_ps"], 1)
                for h in range(H):
                    mm = pe.transpose(bank(6 + h // 4)[:, h % 4], ks[:, h], t.ident[:])
                mm.then_inc(s["ktok_ps"], 1)
                pe.wait_ge(s["diff_done"], 5 * n + 5)
                for h in range(H):
                    mm = pe.transpose(bank(0 + h // 4)[:, h % 4], vs[:, h], t.ident[:])
                mm.then_inc(s["vtok_ps"], 1)
                pe.wait_ge(s["m_done"], 2 * n + 2)
                for h in range(H):
                    mm = pe.transpose(bank(2 + h // 4)[:, h % 4], m_[:, h], t.ident[:])
                mm.then_inc(s["mt_ps"], 1)
                pe.wait_ge(s["tok_done"], n + 1)
                for k in range(1, LEVELS):
                    pe.wait_ge(s["level_masked"], 6 * n + k)
                    for u in range(2):
                        pe.wait_ge(s["x_done"], 13 * n + 1 + (2 * (k - 2) + u + 1 if k > 1 else 0))
                        half_products(4, u, lev[:, k % 2], x_).then_inc(s["p_ps"], 1)
                    for u in range(2):
                        pe.wait_ge(s["p_copied"], 12 * n + 2 * (k - 1) + u + 1)
                        if k < LEVELS - 1:
                            half_products(6, u, xt, pm)
                        half_products(0, u, pm, xt).then_inc(s["q_ps"], 1)
                for u in range(2):
                    pe.wait_ge(s["x_done"], 13 * n + 1 + 11 + u + 0 * n)
                    half_products(4, u, kbe, xt).then_inc(s["w_ps"], 1)
                pe.wait_ge(s["state_scaled"], 2 * n + 1)
                if not first:
                    pe.wait_ge(s["state_in"], 16 * (r + 1))
                for u in range(2):
                    pe.wait_ge(s["w_copied"], 2 * n + u + 1)
                    for h in range(4 * u, 4 * u + 4):
                        pe.matmul(bank(2 + u)[:, h % 4], xt[:, h], vn[:, h], start=True, stop=False)
                        mm = pe.matmul(bank(2 + u)[:, h % 4], wt[:, h], st[:, h], start=False, stop=True)
                    mm.then_inc(s["vn_ps"], 1)
                pe.wait_ge(s["qd_done"], n + 1)
                for u in range(2):
                    pe.wait_ge(s["vn_copied"], 2 * n + u + 1)
                    for h in range(4 * u, 4 * u + 4):
                        pe.matmul(bank(4 + u)[:, h % 4], qd[:, h], st[:, h], start=True, stop=False)
                        mm = pe.matmul(bank(4 + u)[:, h % 4], qk[:, h], vn[:, h], start=False, stop=True)
                    mm.then_inc(s["o_ps"], 1)
                    half_products(6, u, kd, vn).then_inc(s["s_ps"], 1)
            each_batch(pe, batch)

        @block.vector
        def _(dve):
            dve.sem_inc(s["batch_done"], 1)
            step = Chain(dve, s["x_step"])

            def batch(r, b, n, first):
                last = P - 1 if r == 0 else 0
                gate = lambda ap, u, w: ap[:, b, 8 * r + u:8 * r + u + w]
                dve.wait_ge(s["er_done"], n + 1)
                for u in range(2):
                    for out, mask, op in ((m_, above, ALU.max), (qk, below, ALU.min)):
                        for h in range(4 * u, 4 * u + 4):
                            ins = nc.vector.scalar_tensor_tensor(
                                out=out[:, h], in0=bank(h // 4)[:, h % 4], scalar=gate(t.log_decay, h, 1),
                                in1=mask[:, r, :], op0=ALU.subtract, op1=op)
                        ins.then_inc(s["diff_done"], 1)
                nc.vector.tensor_tensor(tail, banks(0)[:, :, last], gate(t.log_decay, 0, 8),
                                        ALU.subtract).then_inc(s["diff_done"], 1)
                dve.wait_ge(s["gram_ps"], n + 1)
                for u in range(2):
                    dve.wait_ge(s["exp_done"], 5 * n + 2 * u + 1)
                    for h in range(4 * u, 4 * u + 4):
                        ins = nc.vector.scalar_tensor_tensor(
                            out=m_[:, h], in0=bank(2 + h // 4)[:, h % 4], scalar=gate(t.beta, h, 1),
                            in1=m_[:, h], op0=ALU.mult, op1=ALU.mult)
                    ins.then_inc(s["m_done"], 1)
                dve.wait_ge(s["m_done"], 2 * n + 2)
                step.sig(nc.vector.tensor_tensor(x_, m_, over(nmask[:, r, 0], H), ALU.mult))
                dve.wait_ge(s["exp_done"], 5 * n + 5)
                dve.wait_ge(s["ktok_ps"], n + 1)
                nc.vector.tensor_tensor(kbe, banks(6), wide(gate(t.beg, 0, 8), P), ALU.mult)
                nc.vector.tensor_tensor(kd, banks(6), wide(tail, P), ALU.mult)
                dve.wait_ge(s["kq_ps"], n + 1)
                nc.vector.tensor_tensor(qk, banks(4), qk, ALU.mult)
                dve.wait_ge(s["vtok_ps"], n + 1)
                nc.vector.tensor_tensor(vn, banks(0), wide(gate(t.beta, 0, 8), P), ALU.mult).then_inc(s["tok_done"], 1)
                dve.wait_ge(s["mt_copied"], 2 * n + 2)
                step.sig(nc.vector.tensor_tensor(xt, mt, over(nmask[:, 1 - r, 0], H), ALU.mult))
                step.sync()
                nc.vector.tensor_tensor(x_, x_, over(t.ident[:], H), ALU.add)
                nc.vector.tensor_tensor(xt, xt, over(t.ident[:], H), ALU.add).then_inc(s["x_done"], 1)
                for k in range(1, LEVELS):
                    for u in range(2):
                        dve.wait_ge(s["q_ps"], 12 * n + 2 * (k - 1) + u + 1)
                        dve.wait_ge(s["x_done"], 13 * n + 1 + 2 * (k - 1))
                        if k < LEVELS - 1:
                            nc.vector.tensor_tensor(half(x_, u), half(x_, u), bank(6 + u), ALU.add)
                        nc.vector.tensor_tensor(half(xt, u), half(xt, u), bank(0 + u), ALU.add).then_inc(s["x_done"], 1)
                for u in range(2):
                    out = half(o_all[:, b], u)
                    dve.wait_ge(s["o_ps"], 2 * n + u + 1)
                    if r == 0:
                        nc.vector.tensor_copy(out, bank(4 + u))
                    else:
                        nc.vector.tensor_tensor(out, out, bank(4 + u), ALU.add)
                dve.wait_ge(s["state_scaled"], 2 * n + 2)
                dve.wait_ge(s["s_ps"], 2 * n + 2)
                nc.vector.tensor_tensor(st, st2, banks(6), ALU.add).then_inc(s["batch_done"], 1)

            for r in range(2):
                step.base = 10 * r
                step.count = 0
                batch(r, 0, 5 * r, True)
                with dve.Fori(0, NB - 1) as j:
                    step.enter(j, 2)
                    batch(r, j + 1 if r == 0 else j * -1 + (NB - 1), 5 * r + 1 + j, False)
                    step.leave(NB - 1)

        @block.scalar
        def _(act):
            def batch(r, b, n, first):
                act.wait_ge(s["decay_ps"], n + 1)
                nc.scalar.activation(qd, banks(0), ACT.Exp).then_inc(s["er_done"], 1)
                for u in range(2):
                    act.wait_ge(s["diff_done"], 5 * n + 2 * u + 1)
                    nc.scalar.activation(half(m_, u), half(m_, u), ACT.Exp, scale=-1.0).then_inc(s["exp_done"], 1)
                    act.wait_ge(s["diff_done"], 5 * n + 2 * u + 2)
                    nc.scalar.activation(half(qk, u), half(qk, u), ACT.Exp).then_inc(s["exp_done"], 1)
                act.wait_ge(s["diff_done"], 5 * n + 5)
                nc.scalar.activation(tail, tail, ACT.Exp).then_inc(s["exp_done"], 1)
                act.wait_ge(s["mt_ps"], n + 1)
                for u in range(2):
                    nc.scalar.activation(half(mt, u), bank(2 + u), ACT.Copy).then_inc(s["mt_copied"], 1)
                for k in range(1, LEVELS):
                    for u in range(2):
                        act.wait_ge(s["p_ps"], 12 * n + 2 * (k - 1) + u + 1)
                        nc.scalar.activation(half(pm, u), bank(4 + u), ACT.Copy).then_inc(s["p_copied"], 1)
                for u in range(2):
                    act.wait_ge(s["w_ps"], 2 * n + u + 1)
                    nc.scalar.activation(half(wt, u), bank(4 + u), ACT.Copy, scale=-1.0).then_inc(s["w_copied"], 1)
                for u in range(2):
                    act.wait_ge(s["vn_ps"], 2 * n + u + 1)
                    nc.scalar.activation(half(vn, u), bank(2 + u), ACT.Copy).then_inc(s["vn_copied"], 1)
            each_batch(act, batch)



def branches(nc, t, a):
    h = t.hx[:].rearrange("p (k n) -> p k n", k=KD)
    o = t.d[:, 0:NB * HD].rearrange("p (b h n) -> p b h n", b=NB, h=H)
    on = t.c[:, 0:H * NT].rearrange("p (h n) -> p h n", h=H)
    vg = t.c[:, H * NT:2 * H * NT].rearrange("p (b n) -> p b n", b=NB)
    gm = t.c[:, 2 * H * NT:3 * H * NT].rearrange("p (h n) -> p h n", h=H)
    w = [t.d[:, 5120 + i * NT:5120 + (i + 1) * NT] for i in range(4)]
    act_out, staged = w[0:2], [x.rearrange("p (b n) -> p b n", b=NB) for x in w[2:4]]
    sq = t.d[:, 7680:7680 + HD]
    gm_norm = t.d[:, 8704:8704 + HD]
    ws = t.d[:, 9728:9728 + HD].rearrange("p (g n) -> p g n", g=H)
    bs = t.d[0:1, 10752:10752 + HD].rearrange("p (g n) -> p g n", g=H)
    so = t.stat[:, 0:40].rearrange("p (b h) -> p b h", b=NB)
    sv = t.stat[:, 40:45]
    (gm_in, o_step, o_root, oT_ps, oT_read, z_read, o_staged, vg_bank, vg_done, vg_step, v_staged, mix_ps,
     mix_read) = (t.sem("br_" + n) for n in (
         "gm_in", "o_step", "o_root", "oT_ps", "oT_read", "z_read", "o_staged", "vg_bank", "vg_done",
         "vg_step", "v_staged", "mix_ps", "mix_read"))

    with nc.Block() as block:
        @block.sync
        def _(sp):
            sp.dma_start(gm_norm, a["gm_norm"].partition_broadcast(P)).then_inc(gm_in, 16)
            sp.dma_start(t.d[:, 9728:9728 + HD], a["gm_w_s"]).then_inc(gm_in, 16)
            sp.dma_start(t.d[0:1, 10752:10752 + HD], a["gm_b_s"]).then_inc(gm_in, 16)
            stream(sp, t, a["w_z"], H)
            t.tiles += H
            stream(sp, t, a["w_vg"], 8)
            t.tiles += 8
            stream(sp, t, a["w_u"], H)
            t.tiles -= H + 8

        @block.gpsimd
        def _(pool):
            pool.wait_ge(o_step, 2 * NB + 2)
            with pool.Fori(0, H // 2) as i:
                for j in range(2):
                    pool.wait_ge(oT_ps, 2 * i + j + 1)
                    nc.gpsimd.tensor_tensor(staged[j], o[:, :, 2 * i + j, :],
                                            so[:, :, bass.ds(2 * i + j, 1)].to_broadcast([P, NB, P]),
                                            ALU.mult).then_inc(o_staged, 1)
            pool.wait_ge(oT_ps, H + 2)
            pool.wait_ge(vg_step, 2 * NB + 2)
            with pool.Fori(0, H // 2) as i:
                for j in range(2):
                    pool.wait_ge(mix_ps, 2 * i + j + 1)
                    nc.gpsimd.tensor_copy(staged[j], vg[:, :, bass.ds((2 * i + j) * P, P)]).then_inc(v_staged, 1)

        @block.tensor
        def _(pe):
            pe.sem_inc(oT_ps, 2)
            with pe.Fori(0, 2) as i:
                for j in range(4):
                    n = 4 * i + j
                    pe.wait_ge(z_read, n + 1)
                    tile_full(pe, t, j, i)
                    project(pe, t, j % 2, t.ring[:, j, :], h).then_inc(t.tile_done, 1)
                    pe.wait_ge(oT_read, n + 1)
                    pe.wait_ge(o_staged, n + 1)
                    for b in range(NB):
                        q = 4 + 2 * (j % 2)
                        out = t.ps[:, q, (b - 1) * P:b * P] if b else t.ps[:, q + 1, 0:P]
                        mm = pe.transpose(out, staged[j % 2][:, b], t.ident[:])
                    mm.then_inc(oT_ps, 1)
            t.tiles += H
            pe.wait_ge(z_read, H + 2)
            pe.wait_ge(oT_read, H + 2)
            with pe.Fori(0, 2) as c:
                for kq in range(4):
                    tile_full(pe, t, kq, c)
                    for b in range(NB):
                        if kq == 0:
                            pe.wait_ge(vg_done, NB * c + b + 1)
                        for kk in range(4):
                            k = 4 * kq + kk
                            mm = pe.matmul(t.ps[:, b, :], h[:, k, b * P:(b + 1) * P],
                                           t.ring[:, kq, kk * COL:(kk + 1) * COL],
                                           start=(k == 0), stop=(k == KD - 1))
                        if kq == 3 and b < NB - 1:
                            mm.then_inc(vg_bank, 1)
                    mm.then_inc(t.tile_done, 1)
            t.tiles += 8
            pe.sem_inc(mix_ps, 2)
            pe.wait_ge(vg_done, 3 * NB)
            pe.wait_ge(gm_in, 48)
            with pe.Fori(0, 2) as i:
                for j in range(4):
                    n = 4 * i + j
                    pe.wait_ge(z_read, H + n + 1)
                    tile_full(pe, t, j, i)
                    project(pe, t, j % 2, t.ring[:, j, :], h).then_inc(t.tile_done, 1)
                    pe.wait_ge(mix_read, n + 1)
                    pe.wait_ge(v_staged, n + 1)
                    q = 4 + 2 * (j % 2)
                    for b in range(NB):
                        out = t.ps[:, q, (b - 1) * P:b * P] if b else t.ps[:, q + 1, 0:P]
                        pe.matmul(out, staged[j % 2][:, b], ws[:, n, :], start=True, stop=False)
                        mm = pe.matmul(out, t.ones[0:1, :], bs[:, n, :], start=False, stop=True)
                    mm.then_inc(mix_ps, 1)
            t.tiles -= H + 8

        @block.vector
        def _(dve):
            for b in range(NB):
                if b:
                    dve.wait_ge(o_step, 2 * b)
                nc.vector.tensor_tensor(sq, t.d[:, b * HD:(b + 1) * HD], t.d[:, b * HD:(b + 1) * HD],
                                        ALU.mult).then_inc(o_step, 1)
                dve.wait_ge(o_step, 2 * b + 1)
                nc.vector.tensor_reduce(so[:, b, :], sq.rearrange("p (h n) -> p h n", h=H), AX_X,
                                        ALU.add).then_inc(o_step, 1)
            dve.wait_ge(o_step, 2 * NB)
            nc.vector.tensor_scalar(so, so, 1.0 / P, EPS, ALU.mult, ALU.add).then_inc(o_step, 1)
            dve.wait_ge(o_root, 1)
            nc.vector.reciprocal(so, so).then_inc(o_step, 1)
            dve.sem_inc(oT_read, 2)
            dve.sem_inc(mix_read, 2)
            with dve.Fori(0, H // 2) as i:
                for j in range(2):
                    n, q = 2 * i + j, 4 + 2 * j
                    dve.wait_ge(z_read, n + 3)
                    dve.wait_ge(oT_ps, n + 3)
                    nc.vector.scalar_tensor_tensor(out=on[:, n, P:NT], in0=t.ps[:, q, :], scalar=t.dn_norm,
                                                   in1=act_out[j][:, P:NT], op0=ALU.mult, op1=ALU.mult)
                    nc.vector.scalar_tensor_tensor(out=on[:, n, 0:P], in0=t.ps[:, q + 1, 0:P], scalar=t.dn_norm,
                                                   in1=act_out[j][:, 0:P], op0=ALU.mult,
                                                   op1=ALU.mult).then_inc(oT_read, 1)
            dve.wait_ge(vg_done, 3 * NB)
            for b in range(NB):
                if b:
                    dve.wait_ge(vg_step, b)
                nc.vector.tensor_tensor_reduce(sq, vg[:, b, :], vg[:, b, :], 1.0, 0.0, ALU.mult, ALU.add,
                                               sv[:, b:b + 1]).then_inc(vg_step, 1)
            dve.wait_ge(vg_step, NB)
            nc.vector.tensor_scalar(sv, sv, 1.0 / HD, EPS, ALU.mult, ALU.add).then_inc(vg_step, 1)
            dve.wait_ge(o_root, 2)
            nc.vector.reciprocal(sv, sv).then_inc(vg_step, 1)
            dve.wait_ge(vg_step, NB + 2)
            dve.wait_ge(gm_in, 48)
            for b in range(NB):
                nc.vector.scalar_tensor_tensor(out=vg[:, b, :], in0=vg[:, b, :], scalar=sv[:, b:b + 1], in1=gm_norm,
                                               op0=ALU.mult, op1=ALU.mult).then_inc(vg_step, 1)
            with dve.Fori(0, H // 2) as i:
                for j in range(2):
                    n, q = 2 * i + j, 4 + 2 * j
                    dve.wait_ge(z_read, H + n + 3)
                    dve.wait_ge(mix_ps, n + 3)
                    nc.vector.tensor_tensor(gm[:, n, P:NT], t.ps[:, q, :], act_out[j][:, P:NT], ALU.mult)
                    nc.vector.tensor_tensor(gm[:, n, 0:P], t.ps[:, q + 1, 0:P], act_out[j][:, 0:P],
                                            ALU.mult).then_inc(mix_read, 1)

        @block.scalar
        def _(act):
            def both(j, fn):
                nc.scalar.activation(act_out[j][:, P:NT], t.ps[:, 2 * j, :], fn)
                nc.scalar.activation(act_out[j][:, 0:P], t.ps[:, 2 * j + 1, 0:P], fn).then_inc(z_read, 1)

            act.sem_inc(z_read, 2)
            act.sem_inc(vg_done, NB)
            act.wait_ge(o_step, 2 * NB + 1)
            nc.scalar.activation(so, so, ACT.Sqrt).then_inc(o_root, 1)
            with act.Fori(0, H // 2) as i:
                for j in range(2):
                    act.wait_ge(t.tile_done, done_count(t, 2 * i + j))
                    act.wait_ge(oT_read, 2 * i + j + 1)
                    both(j, ACT.Silu)
            t.tiles += H
            with act.Fori(0, 2) as c:
                for b in range(NB):
                    if b < NB - 1:
                        act.wait_ge(vg_bank, (NB - 1) * c + b + 1)
                    else:
                        act.wait_ge(t.tile_done, done_count(t, 4 * c + 3))
                    nc.scalar.activation(vg[:, b, bass.ds(c * COL, COL)], t.ps[:, b, :],
                                         ACT.Gelu_apprx_tanh).then_inc(vg_done, 1)
            act.wait_ge(vg_step, NB + 1)
            nc.scalar.activation(sv, sv, ACT.Sqrt).then_inc(o_root, 1)
            t.tiles += 8
            act.wait_ge(oT_read, H + 2)
            with act.Fori(0, H // 2) as i:
                for j in range(2):
                    act.wait_ge(t.tile_done, done_count(t, 2 * i + j))
                    act.wait_ge(mix_read, 2 * i + j + 1)
                    both(j, ACT.Gelu_apprx_tanh)
            t.tiles -= H + 8
    t.tiles += 2 * H + 8



def merge(nc, t, a):
    h = t.hx[:].rearrange("p (k n) -> p k n", k=KD)
    on = t.c[:, 0:H * NT].rearrange("p (h n) -> p h n", h=H)
    gm = t.c[:, 2 * H * NT:3 * H * NT].rearrange("p (h n) -> p h n", h=H)
    merged = t.d[:, 0:KD * NT].rearrange("p (k n) -> p k n", k=KD)
    sig = [t.d[:, KD * NT + i * NT:KD * NT + (i + 1) * NT] for i in range(2)]
    other = t.e[:, 0:NT]
    gate_done, part_done, part_step = t.sem("mg_gate_done"), t.sem("mg_part_done"), t.sem("mg_part_step")

    def parts(pair, out):
        return ((t.ps[:, 2 * pair, :], out[:, P:NT]), (t.ps[:, 2 * pair + 1, 0:P], out[:, 0:P]))

    with nc.Block() as block:
        @block.sync
        def _(sp):
            with sp.Fori(0, KD) as n:
                for s, name in enumerate(("w_ga", "w_a", "w_gb", "w_b")):
                    load_tile(sp, t, a[name], 4 * n + s, s, n)

        @block.tensor
        def _(pe):
            with pe.Fori(0, KD) as n:
                for s, (x, chunks) in enumerate(((h, KD), (on, H), (h, KD), (gm, H))):
                    pe.wait_ge(gate_done if s % 2 == 0 else part_done, 2 * n + s // 2 + 1)
                    tile_full(pe, t, s, n)
                    project(pe, t, s, t.ring[:, s, :], x, chunks).then_inc(t.tile_done, 1)

        @block.scalar
        def _(act):
            act.sem_inc(gate_done, 2)
            with act.Fori(0, KD) as n:
                for u in range(2):
                    act.wait_ge(t.tile_done, done_count(t, 4 * n + 2 * u))
                    act.wait_ge(part_done, 2 * n + u + 1)
                    (x, o), (xc, oc) = parts(2 * u, sig[u])
                    nc.scalar.activation(o, x, ACT.Sigmoid)
                    nc.scalar.activation(oc, xc, ACT.Sigmoid).then_inc(gate_done, 1)

        @block.vector
        def _(dve):
            dve.sem_inc(part_done, 2)
            dve.sem_inc(part_step, 1)
            with dve.Fori(0, KD) as n:
                for u, dst in ((0, merged[:, n]), (1, other)):
                    dve.wait_ge(t.tile_done, done_count(t, 4 * n + 2 * u + 1))
                    dve.wait_ge(gate_done, 2 * n + u + 3)
                    if u:
                        dve.wait_ge(part_step, n + 1)
                    for (x, g), o in zip(parts(2 * u + 1, sig[u]), (dst[:, P:NT], dst[:, 0:P])):
                        ins = nc.vector.tensor_tensor(o, x, g, ALU.mult)
                    ins.then_inc(part_done, 1)
                    if not u:
                        dve.wait_ge(part_done, 2 * n + 3)
                dve.wait_ge(part_done, 2 * n + 4)
                nc.vector.tensor_tensor(merged[:, n], merged[:, n], other, ALU.add).then_inc(part_step, 1)
            dve.wait_ge(part_step, KD + 1)
    t.tiles += 4 * KD



def output_projection(nc, t, a):
    merged = t.d[:, 0:KD * NT].rearrange("p (k n) -> p k n", k=KD)
    x = t.hx[:].rearrange("p (b n) -> p b n", b=NB)
    gt = t.c[:, 0:2 * D].rearrange("p (c n) -> p c n", c=2)
    pos = t.c[:, 2 * D:6 * D].rearrange("p (b n) -> p b n", b=NB - 1)
    part = t.c[:, 6 * D:6 * D + NB * COL].rearrange("p (b n) -> p b n", b=NB)
    norm, scale_lat, shift_lat = t.e[:, 0:D], t.e[:, D:2 * D], t.d[:, 5 * D:6 * D]
    scale_ctx = t.c[:, 5 * D:6 * D]
    x2_in, gt_in, norm_in, ctx_in = (t.sem("op_" + n) for n in ("x_in", "gt_in", "norm_in", "ctx_in"))
    pos_added, bank_done, part_done, part_added = (t.sem("op_" + n) for n in (
        "pos_added", "bank_done", "part_done", "part_added"))
    row = lambda m, c: t.mod_rows[c:c + 1, m * D:(m + 1) * D].partition_broadcast(P)

    with nc.Block() as block:
        @block.sync
        def _(sp):
            stream(sp, t, a["w_out"], KD)

        @block.scalar
        def _(act):
            for b in range(NB):
                act.dma_start(x[:, b], a["x"][b]).then_inc(x2_in, 16)
            for b in range(NB - 1):
                act.dma_start(pos[:, b], a["c_pos"][b]).then_inc(x2_in, 16)
            for c in range(2):
                act.dma_start(gt[:, c], row(GT1, c)).then_inc(gt_in, 16)
            act.dma_start(norm, a["norm_ffn"].partition_broadcast(P)).then_inc(norm_in, 16)
            act.dma_start(scale_lat, row(SC2, 1)).then_inc(norm_in, 16)
            act.dma_start(shift_lat, row(SH2, 1)).then_inc(norm_in, 16)
            act.wait_ge(pos_added, NB - 1)
            act.dma_start(scale_ctx, row(SC2, 0)).then_inc(ctx_in, 16)

        @block.tensor
        def _(pe):
            with pe.Fori(0, 4) as c:
                for kq in range(4):
                    tile_full(pe, t, kq, c)
                    for b in range(NB):
                        if kq == 0:
                            pe.wait_ge(part_done, NB * c + b + 1)
                        for kk in range(4):
                            k = 4 * kq + kk
                            mm = pe.matmul(t.ps[:, b, :], merged[:, k, b * P:(b + 1) * P],
                                           t.ring[:, kq, kk * COL:(kk + 1) * COL],
                                           start=(k == 0), stop=(k == KD - 1))
                        if kq == 3 and b < NB - 1:
                            mm.then_inc(bank_done, 1)
                    mm.then_inc(t.tile_done, 1)

        @block.vector
        def _(dve):
            dve.sem_inc(part_done, NB)
            dve.wait_ge(x2_in, 16 * (2 * NB - 1))
            for b in range(NB - 1):
                nc.vector.tensor_tensor(x[:, b + 1], x[:, b + 1], pos[:, b], ALU.add).then_inc(pos_added, 1)
            dve.wait_ge(norm_in, 48)
            nc.vector.scalar_tensor_tensor(out=scale_lat, in0=scale_lat, scalar=1.0, in1=norm, op0=ALU.add,
                                           op1=ALU.mult)
            dve.wait_ge(ctx_in, 16)
            nc.vector.scalar_tensor_tensor(out=scale_ctx, in0=scale_ctx, scalar=1.0, in1=norm, op0=ALU.add,
                                           op1=ALU.mult)
            dve.wait_ge(gt_in, 32)
            with dve.Fori(0, 4) as c:
                for b in range(NB):
                    if b < NB - 1:
                        dve.wait_ge(bank_done, (NB - 1) * c + b + 1)
                    else:
                        dve.wait_ge(t.tile_done, done_count(t, 4 * c + 3))
                    dve.wait_ge(part_added, NB * c + b + 1)
                    nc.vector.tensor_tensor(part[:, b], t.ps[:, b, :], gt[:, min(b, 1), bass.ds(c * COL, COL)],
                                            ALU.mult).then_inc(part_done, 1)

        @block.gpsimd
        def _(pool):
            pool.sem_inc(part_added, NB)
            with pool.Fori(0, 4) as c:
                for b in range(NB):
                    pool.wait_ge(part_done, NB * c + b + 1 + NB)
                    cols = x[:, b, bass.ds(c * COL, COL)]
                    nc.gpsimd.tensor_tensor(cols, cols, part[:, b], ALU.add).then_inc(part_added, 1)
    t.tiles += KD



def expert_input(nc, t, a):
    x = t.hx[:].rearrange("p (b n) -> p b n", b=NB)
    h2 = t.c[:, 0:NB * D].rearrange("p (b n) -> p b n", b=NB)
    h2t = t.d[:, 0:KD * NT].rearrange("p (k n) -> p k n", k=KD)
    scale = (t.c[:, 5 * D:6 * D], t.e[:, D:2 * D])
    shift = (t.c[:, 6 * D:7 * D], t.d[:, 5 * D:6 * D])
    ss = t.stat[:, 0:NB]
    ctx_in, sq_done, rstd, scaled, h2_done, turned, copied = (t.sem("ei_" + n) for n in (
        "ctx_in", "sq_done", "rstd", "scaled", "h2_done", "turned", "copied"))
    order = [1, 2, 3, 4, 0]
    with nc.Block() as block:
        @block.sync
        def _(sp):
            sp.dma_start(shift[0], t.mod_rows[0:1, SH2 * D:(SH2 + 1) * D].partition_broadcast(P)).then_inc(ctx_in, 16)

        @block.scalar
        def _(act):
            for b in range(NB):
                nc.scalar.activation(h2[:, b], x[:, b], ACT.Square, accum_out=ss[:, b:b + 1]).then_inc(sq_done, 1)
            act.wait_ge(rstd, 1)
            nc.scalar.activation(ss, ss, ACT.Sqrt).then_inc(rstd, 1)
            for m, b in enumerate(order):
                q = 4 * (m % 2)
                for k in range(4):
                    act.wait_ge(turned, 4 * m + k + 1)
                    nc.scalar.activation(h2t[:, 4 * k:4 * k + 4, b * P:(b + 1) * P],
                                         t.ps[:, q + k, :].rearrange("p (k n) -> p k n", k=4),
                                         ACT.Copy).then_inc(copied, 1)

        @block.vector
        def _(dve):
            dve.wait_ge(sq_done, NB)
            nc.vector.tensor_scalar(ss, ss, 1.0 / D, EPS, ALU.mult, ALU.add).then_inc(rstd, 1)
            dve.wait_ge(rstd, 2)
            nc.vector.reciprocal(ss, ss).then_inc(rstd, 1)
            dve.wait_ge(rstd, 3)
            for b in order:
                nc.vector.scalar_tensor_tensor(out=h2[:, b], in0=x[:, b], scalar=ss[:, b:b + 1],
                                               in1=scale[min(b, 1)], op0=ALU.mult, op1=ALU.mult).then_inc(scaled, 1)

        @block.gpsimd
        def _(pool):
            for m, b in enumerate(order):
                pool.wait_ge(scaled, m + 1)
                if b == 0:
                    pool.wait_ge(ctx_in, 16)
                nc.gpsimd.tensor_tensor(h2[:, b], h2[:, b], shift[min(b, 1)], ALU.add).then_inc(h2_done, 1)

        @block.tensor
        def _(pe):
            for m, b in enumerate(order):
                pe.wait_ge(h2_done, m + 1)
                for k in range(KD):
                    if k % 4 == 0 and m >= 2:
                        pe.wait_ge(copied, 4 * (m - 2) + k // 4 + 1)
                    mm = pe.transpose(t.ps[:, 4 * (m % 2) + k // 4, (k % 4) * P:(k % 4 + 1) * P],
                                      h2[:, b, k * P:(k + 1) * P], t.ident[:])
                    if k % 4 == 3:
                        mm.then_inc(turned, 1)


def routing_views(t):
    values = t.d[:, 10240:10240 + 41 * 32]
    keys = t.d[:, 11552:11552 + 41 * 16].bitcast(mybir.dt.bfloat16)
    return values, keys


def settled(e, t):
    e.sem_inc(t.passed, 1)


def scores(nc, t, a):
    h2t = t.d[:, 0:KD * NT].rearrange("p (k n) -> p k n", k=KD)
    sub_keys = t.e[:, 0:D].rearrange("p (m n) -> p m n", m=2 * H)
    query = [t.e[:, D + i * NT:D + (i + 1) * NT] for i in range(2)]
    rest = t.e[:, D + 2 * NT:D + 3 * NT].rearrange("p (b n) -> p b n", b=NB)
    best = t.c[:, 14336:14336 + NB * TOPK].rearrange("p (b n) -> p b n", b=NB)
    where = t.c[:, 14416:14416 + NB * TOPK].bitcast(U32).rearrange("p (b n) -> p b n", b=NB)
    values, keys = routing_views(t)
    by_half = lambda ap: ap[:, 0:NB * 2 * H * TOPK].rearrange("p (b m n) -> p b m n", b=NB, m=2 * H)
    keys_in, query_done, score_ps, score_read, top_step, top_done = (t.sem("sc_" + n) for n in (
        "keys_in", "query_done", "score_ps", "score_read", "top_step", "top_done"))
    tiles = 2 * H
    with nc.Block() as block:
        @block.sync
        def _(sp):
            sp.dma_start(t.e[:, 0:D], a["sub_keys"]).then_inc(keys_in, 16)
            stream(sp, t, a["w_query"], tiles)

        @block.gpsimd
        def _(pool):
            nc.gpsimd.memset(values[:, 40 * 32:], 0.0)
            nc.gpsimd.memset(keys[:, 40 * 32:], 0.0)

        @block.tensor
        def _(pe):
            def score(n, j):
                pe.wait_ge(query_done, n + 3)
                pe.wait_ge(score_read, n + 1)
                q = 4 + 2 * j
                for b in range(NB):
                    out = t.ps[:, q, (b - 1) * P:b * P] if b else t.ps[:, q + 1, 0:P]
                    mm = pe.matmul(out, query[j][:, b * P:(b + 1) * P], sub_keys[:, n, :], start=True, stop=True)
                mm.then_inc(score_ps, 1)

            def four(i, scored):
                for j in range(4):
                    n = 4 * i + j
                    pe.wait_ge(query_done, n + 1)
                    tile_full(pe, t, j, i)
                    project(pe, t, j % 2, t.ring[:, j, :], h2t).then_inc(t.tile_done, 1)
                    if j in scored:
                        score(n - 1, (j + 1) % 2)

            pe.wait_ge(keys_in, 16)
            four(0, (1, 2, 3))
            with pe.Fori(1, tiles // 4) as i:
                four(i, (0, 1, 2, 3))
            score(tiles - 1, 1)

        @block.scalar
        def _(act):
            act.sem_inc(query_done, 2)
            with act.Fori(0, tiles // 2) as i:
                for j in range(2):
                    n = 2 * i + j
                    act.wait_ge(t.tile_done, done_count(t, n))
                    act.wait_ge(score_read, n + 1)
                    nc.scalar.activation(query[j][:, P:NT], t.ps[:, 2 * j, :], ACT.Copy)
                    nc.scalar.activation(query[j][:, 0:P], t.ps[:, 2 * j + 1, 0:P], ACT.Copy).then_inc(query_done, 1)

        @block.vector
        def _(dve):
            dve.sem_inc(score_read, 2)
            step = Chain(dve, top_step)
            with dve.Fori(0, tiles // 2) as i:
                step.enter(i, 10)
                for j in range(2):
                    n, q = 2 * i + j, 4 + 2 * j
                    row = [t.ps[:, q, (b - 1) * P:b * P] if b else t.ps[:, q + 1, 0:P] for b in range(NB)]
                    dve.wait_ge(score_ps, n + 1)
                    settled(dve, t)
                    for b in range(NB):
                        ins = nc.vector.max(best[:, b, 0:8], row[b])
                    step.step(ins)
                    settled(dve, t)
                    for b in range(NB):
                        nc.vector.max_index(where[:, b, 0:8], best[:, b, 0:8], row[b])
                    for b in range(NB):
                        ins = nc.vector.match_replace(out=rest[:, b], in_to_replace=best[:, b, 0:8],
                                                      in_values=row[b], imm_value=LOWEST)
                    step.step(ins)
                    dve.sem_inc(score_read, 1)
                    settled(dve, t)
                    for b in range(NB):
                        ins = nc.vector.max(best[:, b, 8:16], rest[:, b])
                    step.step(ins)
                    settled(dve, t)
                    for b in range(NB):
                        ins = nc.vector.max_index(where[:, b, 8:16], best[:, b, 8:16], rest[:, b])
                    step.step(ins)
                    nc.vector.tensor_copy(by_half(values)[:, :, n, :], best)
                    step.step(nc.vector.tensor_copy(by_half(keys)[:, :, n, :], where))
                step.leave(tiles // 2)
    t.tiles += tiles



def experts(nc, t, a):
    x = t.hx[:].rearrange("p (b n) -> p b n", b=NB)
    h2 = t.c[:, 0:NB * D].rearrange("p (b n) -> p b n", b=NB)
    diag = t.c[:, 5 * D:6 * D].rearrange("p (e n) -> p e n", e=TOPK)
    total = t.c[:, 6 * D:7 * D]
    u_rows = [t.ring[:, s, :] for s in range(4)]
    v_rows = [t.e[:, 0:D], t.e[:, D:2 * D], t.d[:, 0:D], t.d[:, D:2 * D]]
    gt, norm, h2_block = (t.d[:, i * D:(i + 1) * D] for i in (2, 3, 4))
    values, keys = (ap.rearrange("p (i u n) -> p i u n", u=2, n=TOPK) for ap in routing_views(t))
    w = t.c[:, 7 * D:7 * D + 1024]
    sums = w[:, 0:256].rearrange("p (i j) -> p i j", i=TOPK)
    rest = w[:, 256:512]
    onehot = w[:, 512:1024].rearrange("p (u k j) -> p u k j", u=2, k=TOPK)
    sm = t.cw[:].rearrange("p a b -> p (a b)")
    best, key_pair, expd = sm[:, 0:16], sm[:, 16:48].rearrange("p (u n) -> p u n", u=2), sm[:, 48:64]
    place_f = t.cond[:].rearrange("p k c -> p (k c)").rearrange("p (u n) -> p u n", u=2)
    gate = t.scond[:].rearrange("p k c -> p (k c)").rearrange("p (j n) -> p j n", j=2)
    dots = t.scale1[:].rearrange("p k c -> p (k c)").rearrange("p (j n) -> p j n", j=2)
    weight = t.shift1[:].rearrange("p k c -> p (k c)").rearrange("p (j n) -> p j n", j=2)
    low, total_exp, inv_exp, ss, inv = (t.stat[:, i:i + 1] for i in range(5))
    place = t.place
    s = {n: t.sem("ex_" + n) for n in (
        "norm_in", "gt_in", "routed", "route_step", "exp_done", "u_used", "gate_step", "zeroed", "gelu_done", "weighted",
        "v_used", "added", "h2_staged", "fin_step", "fin_act", "y_done", "y_out")}
    u_full, v_full = [t.sem(f"u_full{i}") for i in range(4)], [t.sem(f"v_full{i}") for i in range(4)]
    row = lambda c: t.mod_rows[c:c + 1, GT2 * D:(GT2 + 1) * D].partition_broadcast(P)

    def each_head(engine, head, before=None, after=None):
        with engine.Fori(0, NB) as b:
            if before:
                before(b)
            with engine.Fori(0, H // 2) as hp:
                for j in range(2):
                    head(j, b * H + hp * 2 + j, b)
            if after:
                after(b)

    with nc.Block() as block:
        @block.sync
        def _(sp):
            sp.dma_start(norm, a["norm_final"].partition_broadcast(P)).then_inc(s["norm_in"], 16)
            sp.dma_start(gt, row(0)).then_inc(s["gt_in"], 16)
            with sp.Fori(0, NB - 1) as b:
                sp.wait_ge(s["y_done"], b + 1)
                sp.dma_start(gt, row(1)).then_inc(s["gt_in"], 16)
                sp.dma_start(a["y"][bass.ds(b * P, P), :], x[:, b, :]).then_inc(s["y_out"], 16)
            sp.wait_ge(s["y_done"], NB)
            sp.dma_start(a["y"][(NB - 1) * P:, :], x[:, NB - 1, :]).then_inc(s["y_out"], 16)
            sp.wait_ge(s["y_out"], 16 * NB)

        @block.gpsimd
        def _(pool):
            def head(j, i, b):
                pool.wait_ge(s["routed"], i + 1)
                for rows, table, full, used in ((u_rows, "peer_u", u_full, s["u_used"]),
                                                (v_rows, "peer_v", v_full, s["v_used"])):
                    for e in range(TOPK):
                        pool.wait_ge(used, i * TOPK + e + 1)
                        settled(pool, t)
                        nc.gpsimd.indirect_dma_start(
                            rows[e % 4], None, a[table],
                            bass.IndirectOffsetOnAxis(ap=t.index[:, j, e:e + 1], axis=0)).then_inc(full[e % 4], 16)
            each_head(pool, head)

        @block.tensor
        def _(pe):
            pe.sem_inc(s["v_used"], 4)

            def head(j, i, b):
                pe.wait_ge(s["weighted"], i + 1)
                pe.wait_ge(s["added"], i + 1)
                for e in range(TOPK):
                    pe.wait_ge(v_full[e % 4], 64 * i + 16 * (e // 4 + 1))
                    for c in range(4):
                        mm = pe.matmul(t.ps[:, 4 * j + c, :], diag[:, e, :], v_rows[e % 4][:, c * COL:(c + 1) * COL],
                                       start=(e == 0), stop=(e == TOPK - 1))
                    mm.then_inc(s["v_used"], 1)
            each_head(pe, head)

        @block.scalar
        def _(act):
            def stage(b):
                act.wait_ge(s["u_used"], b * H * TOPK + 4)
                nc.scalar.activation(h2_block, h2[:, b, :], ACT.Copy).then_inc(s["h2_staged"], 1)

            def head(j, i, b):
                act.wait_ge(s["u_used"], (i + 1) * TOPK + 4)
                nc.scalar.activation(weight[:, j], dots[:, j], ACT.Gelu_apprx_tanh).then_inc(s["gelu_done"], 1)
                softmax_exp(i + 1)

            def softmax_exp(i):
                act.wait_ge(s["route_step"], 10 * i + 6)
                nc.scalar.activation(expd, best, ACT.Exp, bias=low, accum_out=total_exp).then_inc(s["exp_done"], 1)

            def finish(b):
                act.wait_ge(s["fin_step"], 4 * b + 2)
                nc.scalar.activation(x[:, b, :], total, ACT.Square, accum_out=ss).then_inc(s["fin_act"], 1)
                act.wait_ge(s["fin_step"], 4 * b + 3)
                nc.scalar.activation(inv, ss, ACT.Sqrt).then_inc(s["fin_act"], 1)

            softmax_exp(0)
            each_head(act, head, stage, finish)

        @block.vector
        def _(dve):
            dve.sem_inc(s["u_used"], 4)
            dve.sem_inc(s["added"], 2)
            step = Chain(dve, s["route_step"])

            def route(i, j):
                step.sig(nc.vector.tensor_tensor(
                    sums, values[:, i, 0, :].unsqueeze(2).to_broadcast([P, TOPK, TOPK]),
                    values[:, i, 1, :].unsqueeze(1).to_broadcast([P, TOPK, TOPK]), ALU.add))
                step.sync()
                flat = w[:, 0:256]
                settled(dve, t)
                step.step(nc.vector.max(best[:, 0:8], flat))
                settled(dve, t)
                nc.vector.max_index(place[:, 0, 0:8], best[:, 0:8], flat)
                step.step(nc.vector.match_replace(out=rest, in_to_replace=best[:, 0:8], in_values=flat,
                                                  imm_value=LOWEST))
                settled(dve, t)
                step.step(nc.vector.max(best[:, 8:16], rest))
                settled(dve, t)
                step.step(nc.vector.max_index(place[:, 0, 8:16], best[:, 8:16], rest))
                nc.vector.tensor_scalar(place[:, 1, :], place[:, 0, :], 4, None, ALU.logical_shift_right)
                nc.vector.tensor_scalar(low, best[:, 0:1], -1.0, None, ALU.mult)
                step.step(nc.vector.tensor_scalar(place[:, 2, :], place[:, 0, :], 15, None, ALU.bitwise_and))
                step.step(nc.vector.tensor_copy(place_f, place[:, 1:3, :]))
                step.step(nc.vector.tensor_tensor(
                    onehot, place_f.unsqueeze(3).to_broadcast([P, 2, TOPK, TOPK]),
                    t.iota.unsqueeze(1).unsqueeze(1).to_broadcast([P, 2, TOPK, TOPK]), ALU.is_equal))
                step.step(nc.vector.tensor_tensor(
                    onehot, onehot, keys[:, i, :, :].unsqueeze(2).to_broadcast([P, 2, TOPK, TOPK]), ALU.mult))
                step.step(nc.vector.tensor_reduce(key_pair, onehot, AX_X, ALU.add))
                nc.vector.scalar_tensor_tensor(out=t.index[:, j, :], in0=key_pair[:, 0], scalar=float(NKEYS),
                                               in1=key_pair[:, 1], op0=ALU.mult, op1=ALU.add).then_inc(s["routed"], 1)
                dve.wait_ge(s["exp_done"], i + 1)
                gate_step.step(nc.vector.reciprocal(inv_exp, total_exp))
                gate_step.step(nc.vector.tensor_scalar(gate[:, j], expd, inv_exp, None, ALU.mult))

            def head(j, i, b):
                dve.wait_ge(s["h2_staged"], b + 1)
                for e in range(TOPK):
                    dve.wait_ge(u_full[e % 4], 64 * i + 16 * (e // 4 + 1))
                    nc.vector.tensor_tensor_reduce(u_rows[e % 4], u_rows[e % 4], h2_block, 1.0, 0.0, ALU.mult,
                                                   ALU.add, dots[:, j, e:e + 1]).then_inc(s["u_used"], 1)
                gate_step.base, gate_step.count = 3 * i + 2, 0
                dve.wait_ge(s["gelu_done"], i + 1)
                gate_step.step(nc.vector.tensor_tensor(weight[:, j], weight[:, j], gate[:, j], ALU.mult))
                nc.vector.tensor_tensor(diag, over(t.ident[:], TOPK), wide(weight[:, j], P),
                                        ALU.mult).then_inc(s["weighted"], 1)
                step.base, step.count = 10 * i + 10, 0
                route(i + 1, 1 - j)
                dve.wait_ge(s["v_used"], (i + 1) * TOPK + 4)
                nc.vector.tensor_tensor(total, total, t.ps[:, 4 * j:4 * j + 4, :].rearrange("p c n -> p (c n)"),
                                        ALU.add).then_inc(s["added"], 1)
                dve.wait_ge(s["added"], i + 3)

            def finish(b):
                dve.wait_ge(s["gt_in"], 16 * (b + 1))
                nc.vector.tensor_tensor(total, total, gt, ALU.mult).then_inc(s["fin_step"], 1)
                dve.wait_ge(s["fin_step"], 4 * b + 1)
                nc.vector.tensor_tensor(total, total, x[:, b, :], ALU.add).then_inc(s["fin_step"], 1)
                dve.wait_ge(s["fin_act"], 2 * b + 1)
                nc.vector.tensor_scalar(ss, ss, 1.0 / D, EPS, ALU.mult, ALU.add).then_inc(s["fin_step"], 1)
                dve.wait_ge(s["fin_act"], 2 * b + 2)
                nc.vector.reciprocal(inv, inv).then_inc(s["fin_step"], 1)
                dve.wait_ge(s["fin_step"], 4 * b + 4)
                nc.vector.scalar_tensor_tensor(out=x[:, b, :], in0=total, scalar=inv, in1=norm, op0=ALU.mult,
                                               op1=ALU.mult).then_inc(s["y_done"], 1)
                dve.wait_ge(s["y_done"], b + 1)
                nc.vector.memset(total, 0.0).then_inc(s["zeroed"], 1)
                dve.wait_ge(s["zeroed"], b + 2)

            gate_step = Chain(dve, s["gate_step"])
            nc.vector.memset(total, 0.0).then_inc(s["zeroed"], 1)
            route(0, 0)
            dve.wait_ge(s["zeroed"], 1)
            dve.wait_ge(s["norm_in"], 16)
            each_head(dve, head, after=finish)


def build(nc, a):
    with ExitStack() as ctx:
        t = allocate(nc, ctx)
        for phase in (modulation, mixer_input, qkv, deltanet, branches, merge, output_projection, expert_input,
                      scores, experts):
            phase(nc, t, a)



def feature_tiles(w):
    k, n = w.shape
    return np.ascontiguousarray(w.reshape(k // P, P, n // P, P).transpose(2, 1, 0, 3)).reshape(n // P, P, k)


def row_tiles(w):
    n = w.shape[1] // COL
    return np.ascontiguousarray(w.reshape(4, 4, P, n, COL).transpose(3, 0, 2, 1, 4)).reshape(4 * n, P, TILE)


def constants():
    i = np.arange(P)
    ident = np.eye(P, dtype=np.float32)
    tri = np.stack([i[:, None] <= i[None, :], i[:, None] >= i[None, :]], 1).astype(np.float32)
    lower = []
    for level in range(LEVELS):
        b = 2 ** level
        half = (i // b) % 2
        lower.append(-((i[:, None] // (2 * b) == i[None, :] // (2 * b)) & (half[:, None] == 1) & (half[None, :] == 0)).astype(np.float32))
    masks = np.stack([np.stack(lower), np.stack([m.T for m in lower])])
    strict = i[:, None] > i[None, :]
    above = np.stack([np.where(strict, 0, BIG), np.where(strict.T, 0, BIG)])
    below = np.stack([np.where(strict.T | (ident > 0), 0, -BIG), np.where(strict | (ident > 0), 0, -BIG)])
    masks = np.concatenate([masks.transpose(2, 0, 1, 3).reshape(P, -1), above.transpose(1, 0, 2).reshape(P, -1),
                            below.transpose(1, 0, 2).reshape(P, -1)], 1).astype(np.float32)
    small = np.concatenate([np.tile(np.arange(16), (P, 1)), np.tile(np.repeat([P ** -0.5, 1.0], H), (P, 1))], 1)
    tokens = np.arange(LAT)
    quarter = D // 4
    freq = (1.0 / (np.float32(10000.0) ** (np.arange(quarter, dtype=np.float32) / np.float32(quarter)))).astype(np.float32)
    def enc(p):
        ang = p.astype(np.float32)[:, None] * freq
        return np.concatenate([np.sin(ang), np.cos(ang)], 1)
    pos = np.concatenate([enc(tokens // 64), enc(tokens % 64)], 1).astype(np.float32)
    return {"c_ident": ident, "c_tri": tri.reshape(P, 2 * P), "c_masks": masks,
            "c_small": small.astype(np.float32), "c_pos": pos.reshape(NB - 1, P, D)}


def lay_out(i):
    w = i["w_in"][0]
    at = np.cumsum([0, 3 * HD, HD, 4 * H, HD, HD, D, D])
    qkv_w, z_w, gates_w, u_w, vg_w, ga_w, gb_w = (w[:, x:y] for x, y in zip(at[:-1], at[1:]))
    cond = np.stack([i["c_ctx"], i["c"][0]])
    row = lambda x: np.ascontiguousarray(x).reshape(1, -1)
    return {
        "x": np.concatenate([i["x_prompt"].reshape(1, P, D), i["x_sample"].reshape(NB - 1, P, D)]),
        "cond": np.ascontiguousarray(cond.reshape(2, KD, P).transpose(2, 1, 0)),
        "w_mod": row_tiles(i["w_mod"][0]), "b_mod": row(i["b_mod"][0]),
        "norm_mix": np.ascontiguousarray(i["norm_mix"][0].reshape(KD, P).T),
        "w_qkv": feature_tiles(qkv_w), "w_z": feature_tiles(z_w), "w_u": feature_tiles(u_w),
        "w_vg": row_tiles(vg_w), "w_ga": feature_tiles(ga_w), "w_gb": feature_tiles(gb_w),
        "w_gates": np.ascontiguousarray(gates_w.reshape(KD, P, 4 * H).transpose(1, 0, 2)).reshape(P, KD * 4 * H),
        "conv_w": np.ascontiguousarray(i["conv_w"][0].reshape(3, 3 * H, P).transpose(2, 1, 0)).reshape(P, 9 * H),
        "a_log": row(i["dn_a_log"][0]), "dt_bias": row(i["dn_dt_bias"][0]),
        "dn_norm": i["dn_norm"][0].reshape(P, 1),
        "state": i["state_delta"][0, 0],
        "gm_norm": row(i["gm_norm"][0]),
        "gm_w_s": np.ascontiguousarray(i["gm_w_s"][0].transpose(2, 0, 1)).reshape(P, HD),
        "gm_b_s": row(i["gm_b_s"][0]),
        "w_a": feature_tiles(i["w_branch_a"][0]), "w_b": feature_tiles(i["w_branch_b"][0]),
        "w_out": row_tiles(i["w_out"][0]), "norm_ffn": row(i["norm_ffn"][0]),
        "w_query": feature_tiles(i["peer_w_query"][0].reshape(D, D)),
        "sub_keys": np.ascontiguousarray(i["peer_sub_keys"][0].reshape(2 * H, NKEYS, P).transpose(2, 0, 1)).reshape(P, 2 * HD),
        "peer_u": i["peer_u"][0], "peer_v": i["peer_v"][0],
        "norm_final": row(i["norm_final"]),
        **constants(),
    }


OUTS = {"y": (NT, D), "new_state": (2, H, P, P)}


def kernel(**inputs):
    import concourse.bacc as bacc
    from concourse.bass_utils import run_bass_kernel_spmd

    arrays = lay_out({k: np.asarray(v) for k, v in inputs.items()})
    nc = bacc.Bacc("TRN2", target_bir_lowering=False, num_devices=1)
    a = {k: nc.dram_tensor(k, v.shape, F32, kind="ExternalInput").ap() for k, v in arrays.items()}
    a |= {k: nc.dram_tensor(k, v, F32, kind="ExternalOutput").ap() for k, v in OUTS.items()}
    build(nc, a)
    got = run_bass_kernel_spmd(nc, [arrays], core_ids=[0]).results[0]
    y = got["y"]
    return (y[0:P].reshape(1, P, D), y[P:].reshape(1, LAT, D), got["new_state"].reshape(1, 1, 2, H, P, P))
```

```python
from contextlib import ExitStack

import numpy as np

import concourse.bass as bass
from concourse import mybir
from concourse.alu_op_type import AluOpType as ALU

ACT = mybir.ActivationFunctionType
AX_X = mybir.AxisListType.X
F32 = mybir.dt.float32
I32 = mybir.dt.int32
U32 = mybir.dt.uint32

P = 128
D = 2048
KD = D // P
NB = 5
NT = NB * P
LAT = NT - P
H = 8
HD = H * P
NMOD = 6
TOPK = 16
NKEYS = 128
EPS = 1e-6
COL = 512
RING = 4
TILE = 2048
LEVELS = 7
BIG = 1e30
LOWEST = -3.0e38
SH1, SC1, GT1, SH2, SC2, GT2 = range(NMOD)


class Store:
    pass


class Chain:

    def __init__(self, engine, sem):
        self.engine, self.sem, self.base, self.count = engine, sem, 0, 0

    def sig(self, instruction):
        instruction.then_inc(self.sem, 1)
        self.count += 1

    def sync(self):
        self.engine.wait_ge(self.sem, self.base + self.count)

    def step(self, instruction):
        self.sig(instruction)
        self.sync()

    def enter(self, i, per):
        self.outer = (self.base + self.count, per)
        self.base, self.count = self.outer[0] + i * per, 0

    def leave(self, passes):
        before, per = self.outer
        assert self.count == per, (self.count, per)
        self.base, self.count = before + passes * per, 0


def col(ap, i):
    return ap[:, bass.ds(i, 1)]


def wide(ap, n):
    return ap.unsqueeze(2).to_broadcast([P, ap.shape[1], n])


def over(ap, n):
    return ap.unsqueeze(1).to_broadcast([P, n, ap.shape[1]])



def allocate(nc, ctx):
    def sb(name, shape, dtype=F32):
        return ctx.enter_context(nc.sbuf_tensor(f"{name}_sb", [P, *shape], dtype))

    t = Store()
    t.ring = sb("ring", [RING, TILE])
    t.hx = sb("hx", [KD * NT])
    t.c = sb("c_region", [3 * H * NT])
    t.d = sb("d_region", [12288])
    t.e = sb("e_region", [4096])
    t.ident = sb("ident", [P])
    t.tri = sb("tri", [2, P])
    t.ones = sb("ones", [P])
    t.small = sb("small", [64])
    t.cw = sb("cw", [3 * H, 3])
    t.cond = sb("cond", [KD, 2])
    t.scond = sb("scond", [KD, 2])
    t.scale1 = sb("scale1", [KD, 2])
    t.shift1 = sb("shift1", [KD, 2])
    t.beta = sb("beta", [NB, 2 * H])
    t.log_decay = sb("log_decay", [NB, 2 * H])
    t.beg = sb("beg", [NB, 2 * H])
    t.g = sb("g", [NB, 2 * H])
    t.stat = sb("stat", [64])
    t.place = sb("place", [3, TOPK], U32)
    t.index = sb("index", [2, TOPK], I32)
    t.index_v = sb("index_v", [2, TOPK], I32)
    t.gate_rows = sb("gate_rows", [H, P])
    t.ps = ctx.enter_context(nc.psum_tensor("ps", [P, 8, COL], F32))
    t.mod_rows = nc.dram_tensor("mod_rows", (2, NMOD * D), F32).ap()
    t.sem = lambda name: ctx.enter_context(nc.semaphore(name))
    t.full = [t.sem(f"ring_full{s}") for s in range(4)]
    t.tile_done = t.sem("tile_done")
    t.x_in, t.init, t.passed = t.sem("x_in"), t.sem("init"), t.sem("passed")
    t.tiles = 0
    t.eps, t.iota, t.qk_scale, t.dn_norm = t.small[:, 0:1], t.small[:, 1:17], t.small[:, 17:33], t.small[:, 33:34]
    return t


def tile_full(e, t, slot, use):
    e.wait_ge(t.full[slot], 16 * (t.tiles // 4 + use + 1))


def done_count(t, g):
    return t.tiles + g + 5


def load_tile(e, t, src, g, slot, tile):
    e.wait_ge(t.tile_done, t.tiles + g + 1)
    e.dma_start(t.ring[:, slot, 0:src.shape[2]],
                src[bass.ds(tile, 1)].rearrange("a p n -> (a p) n")).then_inc(t.full[slot], 16)


def stream(e, t, src, tiles, first=0):
    with e.Fori(first, tiles // 4) as i:
        for s in range(4):
            load_tile(e, t, src, 4 * i + s, s, 4 * i + s)


def prefetch(e, t, tiles, loads):
    for s, (src, tile) in enumerate(loads):
        load_tile(e, t, src, tiles + s, s, tile)



def modulation(nc, t, a):
    groups = 2 * D // COL
    w_tiles = 4 * groups
    cond_in, bias_in, silu_done = t.sem("cond_in"), t.sem("bias_in"), t.sem("silu_done")
    bank_free, turned = t.sem("mod_bank_free"), t.sem("mod_turned")
    rows = t.c[0:2, KD * NT:KD * NT + 2 * D]
    bias = t.d[0:2, 4 * D:6 * D]
    pos_in, x_done, sumsq, rstd, xn_done = (t.sem(n) for n in ("pos_in", "x_done", "sumsq1", "rstd1", "xn_done"))
    ss, root, inv = t.stat[:, 48:53], t.stat[:, 53:58], t.stat[:, 58:63]
    with nc.Block() as block:
        @block.sync
        def _(sp):
            sp.dma_start(t.cond[:], a["cond"]).then_inc(cond_in, 16)
            sp.dma_start(t.ident[:], a["c_ident"]).then_inc(cond_in, 16)
            sp.dma_start(bias, a["b_mod"][:, 0:2 * D].partition_broadcast(2)).then_inc(bias_in, 16)
            stream(sp, t, a["w_mod"], w_tiles)
            prefetch(sp, t, w_tiles, [(a["w_qkv"], i) for i in range(RING)])

        @block.scalar
        def _(act):
            for b in range(NB):
                act.dma_start(t.c[:, b * D:(b + 1) * D], a["x"][b]).then_inc(t.x_in, 16)
            for b in range(1, NB):
                act.dma_start(t.d[:, (b - 1) * D:b * D], a["c_pos"][b - 1]).then_inc(pos_in, 16)
            act.dma_start(t.tri[:], a["c_tri"]).then_inc(t.x_in, 16)
            act.dma_start(t.small[:, 1:33], a["c_small"]).then_inc(t.x_in, 16)
            act.dma_start(t.small[:, 33:34], a["dn_norm"]).then_inc(t.x_in, 16)
            act.dma_start(t.cw[:], a["conv_w"]).then_inc(t.x_in, 16)
            act.dma_start(t.stat[:, 0:16], a["a_log"].partition_broadcast(P)).then_inc(t.x_in, 16)
            act.dma_start(t.stat[:, 16:32], a["dt_bias"].partition_broadcast(P)).then_inc(t.x_in, 16)
            act.dma_start(t.stat[:, 32:48], a["norm_mix"]).then_inc(t.x_in, 16)
            act.wait_ge(cond_in, 32)
            nc.scalar.activation(t.scond[:], t.cond[:], ACT.Silu).then_inc(silu_done, 1)
            act.wait_ge(t.x_in, 16 * 12)
            for b in range(NB):
                if b:
                    act.wait_ge(x_done, b)
                nc.scalar.activation(t.ps[:, 4:8, :].rearrange("p a n -> p (a n)"), t.c[:, b * D:(b + 1) * D],
                                     ACT.Square, accum_out=ss[:, b:b + 1]).then_inc(sumsq, 1)
                act.wait_ge(sumsq, b + 1)
            act.wait_ge(rstd, 1)
            nc.scalar.activation(root, root, ACT.Sqrt).then_inc(rstd, 1)

        @block.tensor
        def _(pe):
            pe.sem_inc(t.tile_done, 4)
            pe.wait_ge(silu_done, 1)
            with pe.Fori(0, groups // 2) as i:
                for q in range(2):
                    pe.wait_ge(bank_free, 2 * i + q + 1)
                    for kq in range(4):
                        tile_full(pe, t, kq, 2 * i + q)
                        for kk in range(4):
                            k = 4 * kq + kk
                            mm = pe.matmul(t.ps[0:2, q, :], t.scond[:, k, :],
                                           t.ring[:, kq, kk * COL:(kk + 1) * COL],
                                           start=(k == 0), stop=(k == KD - 1))
                        mm.then_inc(t.tile_done, 1)
            pe.wait_ge(bank_free, groups + 2)
            for j in range(2 * KD):
                mm = pe.transpose(t.ps[:, 2, 2 * j:2 * j + 2], rows[:, j * P:(j + 1) * P],
                                  t.ident[0:2, 0:2])
            mm.then_inc(turned, 1)

        @block.vector
        def _(dve):
            nc.vector.memset(t.ones[:], 1.0).then_inc(t.init, 1)
            nc.vector.memset(t.eps, EPS).then_inc(t.init, 1)
            dve.sem_inc(bank_free, 2)
            dve.wait_ge(t.x_in, 16 * 12)
            dve.wait_ge(pos_in, 64)
            for b in range(1, NB):
                x = t.c[:, b * D:(b + 1) * D]
                nc.vector.tensor_tensor(x, x, t.d[:, (b - 1) * D:b * D], ALU.add).then_inc(x_done, 1)
            dve.wait_ge(bias_in, 16)
            with dve.Fori(0, groups // 2) as i:
                for q in range(2):
                    n = 2 * i + q
                    dve.wait_ge(t.tile_done, done_count(t, 4 * n + 3))
                    nc.vector.tensor_tensor(rows[:, bass.ds(n * COL, COL)], t.ps[0:2, q, :],
                                            bias[:, bass.ds(n * COL, COL)], ALU.add).then_inc(bank_free, 1)
            dve.wait_ge(sumsq, NB)
            nc.vector.tensor_scalar(root, ss, 1.0 / D, EPS, ALU.mult, ALU.add).then_inc(rstd, 1)
            dve.wait_ge(rstd, 2)
            nc.vector.reciprocal(inv, root).then_inc(rstd, 1)
            dve.wait_ge(rstd, 3)
            for b in range(NB):
                x = t.c[:, b * D:(b + 1) * D]
                nc.vector.tensor_scalar(x, x, inv[:, b:b + 1], None, ALU.mult).then_inc(xn_done, 1)
            dve.wait_ge(turned, 1)
            nc.vector.tensor_copy(t.shift1[:].rearrange("p k c -> p (k c)"),
                                  t.ps[:, 2, 0:2 * KD]).then_inc(t.init, 1)
            nc.vector.scalar_tensor_tensor(
                out=t.scale1[:], in0=t.ps[:, 2, 2 * KD:4 * KD].rearrange("p (k c) -> p k c", c=2),
                scalar=1.0, in1=wide(t.stat[:, 32:48], 2), op0=ALU.add, op1=ALU.mult).then_inc(t.init, 1)
    t.tiles += w_tiles



def mixer_input(nc, t, a):
    turned = t.sem("xn_turned")
    lat_read, ctx_read = t.sem("lat_bank_read1"), t.sem("ctx_bank_read1")
    with nc.Block() as block:
        @block.vector
        def _(dve):
            dve.sem_inc(lat_read, 2)
            for k in range(KD):
                dve.wait_ge(turned, k + 1)
                nc.vector.tensor_scalar(t.hx[:, k * NT + P:(k + 1) * NT], t.ps[:, 2 * (k % 2), :],
                                        t.scale1[:, k, 1:2], t.shift1[:, k, 1:2],
                                        ALU.mult, ALU.add).then_inc(lat_read, 1)

        @block.scalar
        def _(act):
            act.sem_inc(ctx_read, 2)
            for k in range(KD):
                act.wait_ge(turned, k + 1)
                nc.scalar.activation(t.hx[:, k * NT:k * NT + P], t.ps[:, 2 * (k % 2) + 1, 0:P], ACT.Identity,
                                     bias=t.shift1[:, k, 0:1], scale=t.scale1[:, k, 0:1]).then_inc(ctx_read, 1)

        @block.tensor
        def _(pe):
            for k in range(KD):
                pe.wait_ge(lat_read, k + 1)
                pe.wait_ge(ctx_read, k + 1)
                for b in range(NB):
                    out = t.ps[:, 2 * (k % 2), (b - 1) * P:b * P] if b else t.ps[:, 2 * (k % 2) + 1, 0:P]
                    mm = pe.transpose(out, t.c[:, b * D + k * P:b * D + (k + 1) * P], t.ident[:])
                mm.then_inc(turned, 1)



def project(pe, t, pair, weights, x, chunks=KD):
    for k in range(chunks):
        w = weights[:, k * P:(k + 1) * P]
        pe.matmul(t.ps[:, 2 * pair + 1, 0:P], w, x[:, k, 0:P], start=(k == 0), stop=(k == chunks - 1))
        mm = pe.matmul(t.ps[:, 2 * pair, :], w, x[:, k, P:NT], start=(k == 0), stop=(k == chunks - 1))
    return mm


def qkv(nc, t, a):
    h = t.hx[:].rearrange("p (k n) -> p k n", k=KD)
    y = [t.d[:, i * NT:(i + 1) * NT] for i in range(2)]
    s = [t.d[:, (2 + i) * NT:(3 + i) * NT] for i in range(2)]
    sq, norm = t.d[:, 4 * NT:5 * NT], t.d[:, 5 * NT:6 * NT]
    wg = t.d[:, 6 * NT:6 * NT + KD * 32].rearrange("p (k n) -> p k n", k=KD)
    consts_in = t.sem("gate_w_in")
    conv_step, psum_read = t.sem("conv_step"), t.sem("conv_psum_read")
    silu_done, sq_done, norm_ps, norm_step, qk_done = (t.sem(n) for n in (
        "qkv_silu", "qk_square", "qk_norm_sum", "qk_norm_step", "qk_done"))
    gates_ps, gates, cum_ps = t.sem("gates_psum"), t.sem("gates_step"), t.sem("cumsum_psum")
    tiles, with_norm = 3 * H, 2 * H

    with nc.Block() as block:
        @block.sync
        def _(sp):
            sp.dma_start(wg, a["w_gates"]).then_inc(consts_in, 16)
            sp.dma_start(t.d[:, 5120:5120 + 2304], a["c_masks"]).then_inc(consts_in, 16)
            stream(sp, t, a["w_qkv"], tiles, first=1)

        @block.tensor
        def _(pe):
            def norm_sum(n):
                pe.wait_ge(sq_done, n + 1)
                pe.matmul(t.ps[:, 5, 0:P], t.ones[:], sq[:, 0:P], start=True, stop=True)
                pe.matmul(t.ps[:, 4, :], t.ones[:], sq[:, P:NT], start=True, stop=True).then_inc(norm_ps, 1)

            def four(i, norms):
                for j in range(4):
                    n = 4 * i + j
                    pe.wait_ge(psum_read, n + 1)
                    tile_full(pe, t, j, i)
                    project(pe, t, j % 2, t.ring[:, j, :], h).then_inc(t.tile_done, 1)
                    if j in norms:
                        norm_sum(n - 1)

            four(0, (1, 2, 3))
            with pe.Fori(1, with_norm // 4) as i:
                four(i, (0, 1, 2, 3))
            four(with_norm // 4, (0,))
            four(with_norm // 4 + 1, ())
            pe.wait_ge(consts_in, 32)
            pe.wait_ge(psum_read, tiles + 2)
            for b in range(NB):
                for k in range(KD):
                    mm = pe.matmul(t.ps[:, 6, 32 * b:32 * b + 32], h[:, k, b * P:(b + 1) * P], wg[:, k, :],
                                   start=(k == 0), stop=(k == KD - 1))
            mm.then_inc(gates_ps, 1)
            pe.wait_ge(gates, 7)
            for b in range(NB):
                for r in range(2):
                    o = 16 * b + 8 * r
                    mm = pe.matmul(t.ps[:, 7, o:o + 8], t.tri[:, r, :], t.g[:, b, 8 * r:8 * r + 8],
                                   start=True, stop=True)
            mm.then_inc(cum_ps, 1)

        @block.vector
        def _(dve):
            chain = Chain(dve, conv_step)
            dve.sem_inc(psum_read, 2)

            def conv(n, j):
                out, pair = y[j], j
                w = [t.cw[:, bass.ds(n, 1), k:k + 1].rearrange("p a b -> p (a b)") for k in range(3)]
                seqs = ((t.ps[:, 2 * pair, :], out[:, P:NT]), (t.ps[:, 2 * pair + 1, 0:P], out[:, 0:P]))
                dve.wait_ge(t.tile_done, done_count(t, n))
                dve.wait_ge(silu_done, n + 1)
                for x, o in seqs:
                    chain.sig(nc.vector.tensor_scalar(o, x, w[1], None, ALU.mult))
                chain.sync()
                for x, o in seqs:
                    m = o.shape[1]
                    chain.sig(nc.vector.scalar_tensor_tensor(out=o[:, 1:m], in0=x[:, 0:m - 1], scalar=w[0],
                                                             in1=o[:, 1:m], op0=ALU.mult, op1=ALU.add))
                chain.sync()
                (x, o), (xc, oc) = seqs
                chain.sig(nc.vector.scalar_tensor_tensor(out=o[:, 0:LAT - 1], in0=x[:, 1:LAT], scalar=w[2],
                                                         in1=o[:, 0:LAT - 1], op0=ALU.mult, op1=ALU.add))
                nc.vector.scalar_tensor_tensor(out=oc[:, 0:P - 1], in0=xc[:, 1:P], scalar=w[2],
                                               in1=oc[:, 0:P - 1], op0=ALU.mult,
                                               op1=ALU.add).then_inc(psum_read, 1)

            def normalise(n, j):
                dve.wait_ge(norm_step, 2 * n + 1)
                nc.vector.reciprocal(norm, norm).then_inc(norm_step, 1)
                dve.wait_ge(norm_step, 2 * n + 2)
                nc.vector.scalar_tensor_tensor(out=t.c[:, bass.ds(n * NT, NT)], in0=s[j],
                                               scalar=col(t.qk_scale, n), in1=norm,
                                               op0=ALU.mult, op1=ALU.mult).then_inc(qk_done, 1)

            with dve.Fori(0, with_norm // 2) as i:
                chain.enter(i, 10)
                for j in range(2):
                    conv(2 * i + j, j)
                    normalise(2 * i + j, j)
                chain.leave(with_norm // 2)
            with dve.Fori(with_norm // 2, tiles // 2) as i:
                chain.enter(i - with_norm // 2, 10)
                for j in range(2):
                    conv(2 * i + j, j)
                chain.leave((tiles - with_norm) // 2)

            raw = t.ps[:, 6, 0:32 * NB].rearrange("p (b n) -> p b n", b=NB)
            ab, soft = t.beg[:], t.log_decay[:]
            dve.wait_ge(gates_ps, 1)
            nc.vector.tensor_tensor(ab, raw[:, :, 16:32], over(t.stat[:, 16:32], NB), ALU.add).then_inc(gates, 1)
            dve.wait_ge(gates, 4)
            nc.vector.scalar_tensor_tensor(out=soft, in0=ab, scalar=0.0, in1=soft, op0=ALU.max,
                                           op1=ALU.add).then_inc(gates, 1)
            dve.wait_ge(gates, 6)
            nc.vector.scalar_tensor_tensor(out=t.g[:], in0=soft, scalar=-1.0, in1=over(t.stat[:, 0:16], NB),
                                           op0=ALU.mult, op1=ALU.mult).then_inc(gates, 1)
            dve.wait_ge(cum_ps, 1)
            nc.vector.tensor_copy(t.log_decay[:].rearrange("p a b -> p (a b)"), t.ps[:, 7, 0:80]).then_inc(gates, 1)
            dve.wait_ge(gates, 9)
            nc.vector.tensor_tensor(t.beg[:], t.beg[:], t.beta[:], ALU.mult).then_inc(gates, 1)

        @block.scalar
        def _(act):
            act.sem_inc(silu_done, 2)
            act.sem_inc(qk_done, 2)
            with act.Fori(0, with_norm // 2) as i:
                for j in range(2):
                    n = 2 * i + j
                    act.wait_ge(psum_read, n + 3)
                    act.wait_ge(conv_step, 5 * n + 5)
                    act.wait_ge(qk_done, n + 1)
                    nc.scalar.activation(s[j], y[j], ACT.Silu).then_inc(silu_done, 1)
                    act.wait_ge(silu_done, n + 3)
                    act.wait_ge(qk_done, n + 2)
                    nc.scalar.activation(sq, s[j], ACT.Square).then_inc(sq_done, 1)
                    act.wait_ge(norm_ps, n + 1)
                    nc.scalar.activation(norm[:, P:NT], t.ps[:, 4, :], ACT.Sqrt, bias=t.eps)
                    nc.scalar.activation(norm[:, 0:P], t.ps[:, 5, 0:P], ACT.Sqrt, bias=t.eps).then_inc(norm_step, 1)
            with act.Fori(with_norm // 2, tiles // 2) as i:
                for j in range(2):
                    n = 2 * i + j
                    act.wait_ge(psum_read, n + 3)
                    act.wait_ge(conv_step, 5 * n + 5)
                    nc.scalar.activation(t.c[:, bass.ds(n * NT, NT)], y[j], ACT.Silu).then_inc(silu_done, 1)
            raw = t.ps[:, 6, 0:32 * NB].rearrange("p (b n) -> p b n", b=NB)
            ab, soft = t.beg[:], t.log_decay[:]
            act.wait_ge(gates, 1)
            nc.scalar.activation(soft, ab, ACT.Abs).then_inc(gates, 1)
            act.wait_ge(gates, 2)
            nc.scalar.activation(soft, soft, ACT.Exp, scale=-1.0).then_inc(gates, 1)
            act.wait_ge(gates, 3)
            nc.scalar.activation(soft, soft, ACT.Ln, bias=1.0).then_inc(gates, 1)
            act.wait_ge(gates, 5)
            nc.scalar.activation(t.stat[:, 0:16], t.stat[:, 0:16], ACT.Exp).then_inc(gates, 1)
            nc.scalar.activation(t.beta[:], raw[:, :, 0:16], ACT.Sigmoid)
            act.wait_ge(gates, 8)
            nc.scalar.activation(t.beg[:], t.log_decay[:], ACT.Exp).then_inc(gates, 1)
    t.tiles += tiles



def deltanet(nc, t, a):
    r8 = t.ring[:].rearrange("p s (u h n) -> p (s u) h n", u=2, h=H)
    x_, xt, pm, m_, mt, lev, kbe = (r8[:, i] for i in (0, 1, 2, 3, 4, slice(5, 7), 7))
    e8 = t.e[:].rearrange("p (u h n) -> p u h n", u=4, h=H)
    kd, vn, qd, qk = (e8[:, i] for i in range(4))
    wt, gb = m_, t.gate_rows[:]
    o_all = t.d[:, 0:NB * HD].rearrange("p (b h n) -> p b h n", b=NB, h=H)
    nmask = t.d[:, 5120:6912].rearrange("p (r l n) -> p r l n", r=2, l=LEVELS)
    above = t.d[:, 6912:7168].rearrange("p (r n) -> p r n", r=2)
    below = t.d[:, 7168:7424].rearrange("p (r n) -> p r n", r=2)
    st, st2, ks, vs = (t.d[:, o:o + HD].rearrange("p (h n) -> p h n", h=H) for o in (7424, 8448, 9472, 10496))
    heads = t.c[:].rearrange("p (w n) -> p w n", n=NT)
    tail = t.stat[:, 0:8]

    def bank(i):
        return t.ps[:, i, :].rearrange("p (h n) -> p h n", h=4)

    def banks(i):
        return t.ps[:, i:i + 2, :].rearrange("p u (h n) -> p (u h) n", h=4)

    def half(ap, u):
        return ap[:, 4 * u:4 * u + 4]

    def changed(ap, k, second):
        return ap.rearrange("p h (a t n) -> p h a t n", t=2, n=2 ** k)[:, :, :, second, :]

    def compact(ap, k, side):
        return ap[:, :, side * 64:side * 64 + 64].rearrange("p h (a n) -> p h a n", n=2 ** k)

    s = {n: t.sem("dn_" + n) for n in (
        "decay_ps", "gram_ps", "kq_ps", "ktok_ps", "vtok_ps", "mt_ps", "p_ps", "q_ps", "w_ps", "vn_ps",
        "o_ps", "s_ps",
        "staged", "state_scaled", "qd_done", "level_masked",
        "diff_done", "m_done", "tok_done", "x_done", "x_step", "batch_done",
        "er_done", "exp_done", "mt_copied", "p_copied", "w_copied", "vn_copied",
        "state_out", "state_in")}

    def each_batch(engine, body):
        for r in range(2):
            body(r, 0, 5 * r, True)
            with engine.Fori(0, NB - 1) as j:
                body(r, j + 1 if r == 0 else j * -1 + (NB - 1), 5 * r + 1 + j, False)

    def tokens(ap, b):
        return ap[:, :, bass.ds(b * P, P)]

    with nc.Block() as block:
        @block.sync
        def _(sp):
            for r in range(2):
                sp.wait_ge(s["batch_done"], 5 * r + 2)
                sp.dma_start(a["new_state"][r].rearrange("h d e -> d h e"), st).then_inc(s["state_out"], 16)
                sp.wait_ge(s["state_out"], 16 * (r + 1))
                sp.dma_start(st, a["state"][r].rearrange("h d e -> d h e")).then_inc(s["state_in"], 16)

        @block.gpsimd
        def _(pool):
            def batch(r, b, n, first):
                last = P - 1 if r == 0 else 0
                pool.wait_ge(s["batch_done"], n + 1)
                if first:
                    nc.gpsimd.memset(st, 0.0).then_inc(s["state_scaled"], 1)
                    pool.wait_ge(s["state_scaled"], 2 * n + 1)
                else:
                    pool.wait_ge(s["state_in"], 16 * (r + 1))
                    pool.sem_inc(s["state_scaled"], 1)
                pool.wait_ge(s["er_done"], n + 1)
                nc.gpsimd.tensor_tensor(st2, st, qd[:, :, last:last + 1].to_broadcast([P, H, P]),
                                        ALU.mult).then_inc(s["state_scaled"], 1)
                pool.wait_ge(s["state_scaled"], 2 * n + 2)
                nc.gpsimd.tensor_tensor(qd, qd, tokens(heads[:, 0:8], b), ALU.mult).then_inc(s["qd_done"], 1)
                pool.wait_ge(s["mt_copied"], 2 * n + 2)
                for k in range(1, LEVELS):
                    if k >= 3:
                        pool.wait_ge(s["p_ps"], 12 * n + 2 * (k - 2))
                    nc.gpsimd.tensor_tensor(lev[:, k % 2], mt, over(nmask[:, 1 - r, k], H),
                                            ALU.mult).then_inc(s["level_masked"], 1)

            def stage(r, b):
                nc.gpsimd.tensor_copy(gb, t.g[:, b, 8 * r:8 * r + 8].unsqueeze(2).to_broadcast([P, H, P]))
                nc.gpsimd.tensor_copy(ks, tokens(heads[:, 8:16], b))
                nc.gpsimd.tensor_copy(vs, tokens(heads[:, 16:24], b)).then_inc(s["staged"], 1)

            stage(0, 0)
            for r, at in ((0, lambda j: j + 1), (1, lambda j: j * -1 + (NB - 1))):
                batch(r, 0, 5 * r, True)
                stage(r, at(0))
                with pool.Fori(0, NB - 2) as j:
                    batch(r, at(j), 5 * r + 1 + j, False)
                    stage(r, at(j + 1))
                batch(r, at(NB - 2), 5 * r + NB - 1, False)
                if r == 0:
                    stage(1, 0)

        @block.tensor
        def _(pe):
            def products(out, lhs, rhs):
                for h in range(H):
                    mm = pe.matmul(bank(out + h // 4)[:, h % 4], lhs[:, h], rhs(h), start=True, stop=True)
                return mm

            def half_products(out, u, lhs, rhs):
                for h in range(4 * u, 4 * u + 4):
                    mm = pe.matmul(bank(out + u)[:, h % 4], lhs[:, h], rhs[:, h], start=True, stop=True)
                return mm

            def changed_products(side, u, lhs, rhs, k, second):
                for h in range(4 * u, 4 * u + 4):
                    mm = pe.matmul(compact(bank(2 + u), k, side)[:, h % 4], lhs[:, h], changed(rhs, k, second)[:, h],
                                   start=True, stop=True)
                return mm

            def batch(r, b, n, first):
                pe.wait_ge(s["staged"], n + 1)
                products(0, gb, lambda h: t.tri[:, r, :]).then_inc(s["decay_ps"], 1)
                products(2, ks, lambda h: ks[:, h]).then_inc(s["gram_ps"], 1)
                q = tokens(heads[:, 0:8], b)
                pe.wait_ge(s["batch_done"], n + 1)
                products(4, ks, lambda h: q[:, h]).then_inc(s["kq_ps"], 1)
                for h in range(H):
                    mm = pe.transpose(bank(6 + h // 4)[:, h % 4], ks[:, h], t.ident[:])
                mm.then_inc(s["ktok_ps"], 1)
                pe.wait_ge(s["diff_done"], 5 * n + 5)
                for h in range(H):
                    mm = pe.transpose(bank(0 + h // 4)[:, h % 4], vs[:, h], t.ident[:])
                mm.then_inc(s["vtok_ps"], 1)
                pe.wait_ge(s["m_done"], 2 * n + 2)
                for h in range(H):
                    mm = pe.transpose(bank(2 + h // 4)[:, h % 4], m_[:, h], t.ident[:])
                mm.then_inc(s["mt_ps"], 1)
                pe.wait_ge(s["tok_done"], n + 1)
                for k in range(1, LEVELS):
                    pe.wait_ge(s["level_masked"], 6 * n + k)
                    for u in range(2):
                        pe.wait_ge(s["x_done"], 13 * n + 1 + (2 * (k - 2) + u + 1 if k > 1 else 0))
                        half_products(4, u, lev[:, k % 2], x_).then_inc(s["p_ps"], 1)
                    for u in range(2):
                        pe.wait_ge(s["p_copied"], 12 * n + 2 * (k - 1) + u + 1)
                        if k < LEVELS - 1:
                            changed_products(1, u, xt, pm, k, r)
                        changed_products(0, u, pm, xt, k, 1 - r).then_inc(s["q_ps"], 1)
                for u in range(2):
                    pe.wait_ge(s["x_done"], 13 * n + 1 + 11 + u + 0 * n)
                    half_products(4, u, kbe, xt).then_inc(s["w_ps"], 1)
                pe.wait_ge(s["state_scaled"], 2 * n + 1)
                if not first:
                    pe.wait_ge(s["state_in"], 16 * (r + 1))
                for u in range(2):
                    pe.wait_ge(s["w_copied"], 2 * n + u + 1)
                    for h in range(4 * u, 4 * u + 4):
                        pe.matmul(bank(2 + u)[:, h % 4], xt[:, h], vn[:, h], start=True, stop=False)
                        mm = pe.matmul(bank(2 + u)[:, h % 4], wt[:, h], st[:, h], start=False, stop=True)
                    mm.then_inc(s["vn_ps"], 1)
                pe.wait_ge(s["qd_done"], n + 1)
                for u in range(2):
                    pe.wait_ge(s["vn_copied"], 2 * n + u + 1)
                    for h in range(4 * u, 4 * u + 4):
                        pe.matmul(bank(4 + u)[:, h % 4], qd[:, h], st[:, h], start=True, stop=False)
                        mm = pe.matmul(bank(4 + u)[:, h % 4], qk[:, h], vn[:, h], start=False, stop=True)
                    mm.then_inc(s["o_ps"], 1)
                    half_products(6, u, kd, vn).then_inc(s["s_ps"], 1)
            each_batch(pe, batch)

        @block.vector
        def _(dve):
            dve.sem_inc(s["batch_done"], 1)
            step = Chain(dve, s["x_step"])

            def batch(r, b, n, first):
                last = P - 1 if r == 0 else 0
                gate = lambda ap, u, w: ap[:, b, 8 * r + u:8 * r + u + w]
                dve.wait_ge(s["er_done"], n + 1)
                for u in range(2):
                    for out, mask, op in ((m_, above, ALU.max), (qk, below, ALU.min)):
                        for h in range(4 * u, 4 * u + 4):
                            ins = nc.vector.scalar_tensor_tensor(
                                out=out[:, h], in0=bank(h // 4)[:, h % 4], scalar=gate(t.log_decay, h, 1),
                                in1=mask[:, r, :], op0=ALU.subtract, op1=op)
                        ins.then_inc(s["diff_done"], 1)
                nc.vector.tensor_tensor(tail, banks(0)[:, :, last], gate(t.log_decay, 0, 8),
                                        ALU.subtract).then_inc(s["diff_done"], 1)
                dve.wait_ge(s["gram_ps"], n + 1)
                for u in range(2):
                    dve.wait_ge(s["exp_done"], 5 * n + 2 * u + 1)
                    for h in range(4 * u, 4 * u + 4):
                        ins = nc.vector.scalar_tensor_tensor(
                            out=m_[:, h], in0=bank(2 + h // 4)[:, h % 4], scalar=gate(t.beta, h, 1),
                            in1=m_[:, h], op0=ALU.mult, op1=ALU.mult)
                    ins.then_inc(s["m_done"], 1)
                dve.wait_ge(s["m_done"], 2 * n + 2)
                step.sig(nc.vector.tensor_tensor(x_, m_, over(nmask[:, r, 0], H), ALU.mult))
                dve.wait_ge(s["exp_done"], 5 * n + 5)
                dve.wait_ge(s["kq_ps"], n + 1)
                nc.vector.tensor_tensor(qk, banks(4), qk, ALU.mult).then_inc(s["tok_done"], 1)
                step.sync()
                nc.vector.tensor_tensor(x_, x_, over(t.ident[:], H), ALU.add)
                dve.wait_ge(s["mt_copied"], 2 * n + 2)
                step.sig(nc.vector.tensor_tensor(xt, mt, over(nmask[:, 1 - r, 0], H), ALU.mult))
                step.sync()
                nc.vector.tensor_tensor(xt, xt, over(t.ident[:], H), ALU.add).then_inc(s["x_done"], 1)
                for k in range(1, LEVELS):
                    for u in range(2):
                        dve.wait_ge(s["q_ps"], 12 * n + 2 * (k - 1) + u + 1)
                        dve.wait_ge(s["x_done"], 13 * n + 1 + 2 * (k - 1))
                        if k < LEVELS - 1:
                            cols = changed(half(x_, u), k, r)
                            nc.vector.tensor_tensor(cols, cols, compact(bank(2 + u), k, 1), ALU.add)
                        cols = changed(half(xt, u), k, 1 - r)
                        nc.vector.tensor_tensor(cols, cols, compact(bank(2 + u), k, 0), ALU.add).then_inc(s["x_done"], 1)
                    if k == 1:
                        dve.wait_ge(s["ktok_ps"], n + 1)
                        nc.vector.tensor_tensor(kbe, banks(6), wide(gate(t.beg, 0, 8), P), ALU.mult)
                    elif k == 2:
                        nc.vector.tensor_tensor(kd, banks(6), wide(tail, P), ALU.mult)
                    elif k == 3:
                        dve.wait_ge(s["vtok_ps"], n + 1)
                        nc.vector.tensor_tensor(vn, banks(0), wide(gate(t.beta, 0, 8), P), ALU.mult)
                for u in range(2):
                    out = half(o_all[:, b], u)
                    dve.wait_ge(s["o_ps"], 2 * n + u + 1)
                    if r == 0:
                        nc.vector.tensor_copy(out, bank(4 + u))
                    else:
                        nc.vector.tensor_tensor(out, out, bank(4 + u), ALU.add)
                dve.wait_ge(s["state_scaled"], 2 * n + 2)
                dve.wait_ge(s["s_ps"], 2 * n + 2)
                nc.vector.tensor_tensor(st, st2, banks(6), ALU.add).then_inc(s["batch_done"], 1)

            for r in range(2):
                step.base = 10 * r
                step.count = 0
                batch(r, 0, 5 * r, True)
                with dve.Fori(0, NB - 1) as j:
                    step.enter(j, 2)
                    batch(r, j + 1 if r == 0 else j * -1 + (NB - 1), 5 * r + 1 + j, False)
                    step.leave(NB - 1)

        @block.scalar
        def _(act):
            def batch(r, b, n, first):
                act.wait_ge(s["decay_ps"], n + 1)
                nc.scalar.activation(qd, banks(0), ACT.Exp).then_inc(s["er_done"], 1)
                for u in range(2):
                    act.wait_ge(s["diff_done"], 5 * n + 2 * u + 1)
                    nc.scalar.activation(half(m_, u), half(m_, u), ACT.Exp, scale=-1.0).then_inc(s["exp_done"], 1)
                    act.wait_ge(s["diff_done"], 5 * n + 2 * u + 2)
                    nc.scalar.activation(half(qk, u), half(qk, u), ACT.Exp).then_inc(s["exp_done"], 1)
                act.wait_ge(s["diff_done"], 5 * n + 5)
                nc.scalar.activation(tail, tail, ACT.Exp).then_inc(s["exp_done"], 1)
                act.wait_ge(s["mt_ps"], n + 1)
                for u in range(2):
                    nc.scalar.activation(half(mt, u), bank(2 + u), ACT.Copy).then_inc(s["mt_copied"], 1)
                for k in range(1, LEVELS):
                    for u in range(2):
                        act.wait_ge(s["p_ps"], 12 * n + 2 * (k - 1) + u + 1)
                        nc.scalar.activation(half(pm, u), bank(4 + u), ACT.Copy).then_inc(s["p_copied"], 1)
                for u in range(2):
                    act.wait_ge(s["w_ps"], 2 * n + u + 1)
                    nc.scalar.activation(half(wt, u), bank(4 + u), ACT.Copy, scale=-1.0).then_inc(s["w_copied"], 1)
                for u in range(2):
                    act.wait_ge(s["vn_ps"], 2 * n + u + 1)
                    nc.scalar.activation(half(vn, u), bank(2 + u), ACT.Copy).then_inc(s["vn_copied"], 1)
            each_batch(act, batch)



def branches(nc, t, a):
    h = t.hx[:].rearrange("p (k n) -> p k n", k=KD)
    o = t.d[:, 0:NB * HD].rearrange("p (b h n) -> p b h n", b=NB, h=H)
    on = t.c[:, 0:H * NT].rearrange("p (h n) -> p h n", h=H)
    vg = t.c[:, H * NT:2 * H * NT].rearrange("p (b n) -> p b n", b=NB)
    gm = t.c[:, 2 * H * NT:3 * H * NT].rearrange("p (h n) -> p h n", h=H)
    w = [t.d[:, 5120 + i * NT:5120 + (i + 1) * NT] for i in range(4)]
    act_out, staged = w[0:2], [x.rearrange("p (b n) -> p b n", b=NB) for x in w[2:4]]
    sq = t.d[:, 7680:7680 + HD]
    gm_norm = t.d[:, 8704:8704 + HD]
    ws = t.d[:, 9728:9728 + HD].rearrange("p (g n) -> p g n", g=H)
    bs = t.d[0:1, 10752:10752 + HD].rearrange("p (g n) -> p g n", g=H)
    so = t.stat[:, 0:40].rearrange("p (b h) -> p b h", b=NB)
    sv = t.stat[:, 40:45]
    (gm_in, o_step, o_root, oT_ps, oT_read, z_read, o_staged, vg_bank, vg_done, vg_step, v_staged, mix_ps,
     mix_read) = (t.sem("br_" + n) for n in (
         "gm_in", "o_step", "o_root", "oT_ps", "oT_read", "z_read", "o_staged", "vg_bank", "vg_done",
         "vg_step", "v_staged", "mix_ps", "mix_read"))

    with nc.Block() as block:
        @block.sync
        def _(sp):
            stream(sp, t, a["w_z"], H)
            sp.dma_start(gm_norm, a["gm_norm"].partition_broadcast(P)).then_inc(gm_in, 16)
            sp.dma_start(t.d[:, 9728:9728 + HD], a["gm_w_s"]).then_inc(gm_in, 16)
            sp.dma_start(t.d[0:1, 10752:10752 + HD], a["gm_b_s"]).then_inc(gm_in, 16)
            t.tiles += H
            stream(sp, t, a["w_vg"], 8)
            t.tiles += 8
            stream(sp, t, a["w_u"], H)
            prefetch(sp, t, H, [(a[name], 0) for name in ("w_ga", "w_a", "w_gb", "w_b")])
            t.tiles -= H + 8

        @block.gpsimd
        def _(pool):
            pool.wait_ge(o_step, 2 * NB + 2)
            with pool.Fori(0, H // 2) as i:
                for j in range(2):
                    pool.wait_ge(oT_ps, 2 * i + j + 1)
                    nc.gpsimd.tensor_tensor(staged[j], o[:, :, 2 * i + j, :],
                                            so[:, :, bass.ds(2 * i + j, 1)].to_broadcast([P, NB, P]),
                                            ALU.mult).then_inc(o_staged, 1)
            pool.wait_ge(oT_ps, H + 2)
            pool.wait_ge(vg_step, 2 * NB + 2)
            with pool.Fori(0, H // 2) as i:
                for j in range(2):
                    pool.wait_ge(mix_ps, 2 * i + j + 1)
                    nc.gpsimd.tensor_copy(staged[j], vg[:, :, bass.ds((2 * i + j) * P, P)]).then_inc(v_staged, 1)

        @block.tensor
        def _(pe):
            pe.sem_inc(oT_ps, 2)
            with pe.Fori(0, 2) as i:
                for j in range(4):
                    n = 4 * i + j
                    pe.wait_ge(z_read, n + 1)
                    tile_full(pe, t, j, i)
                    project(pe, t, j % 2, t.ring[:, j, :], h).then_inc(t.tile_done, 1)
                    pe.wait_ge(oT_read, n + 1)
                    pe.wait_ge(o_staged, n + 1)
                    for b in range(NB):
                        q = 4 + 2 * (j % 2)
                        out = t.ps[:, q, (b - 1) * P:b * P] if b else t.ps[:, q + 1, 0:P]
                        mm = pe.transpose(out, staged[j % 2][:, b], t.ident[:])
                    mm.then_inc(oT_ps, 1)
            t.tiles += H
            pe.wait_ge(z_read, H + 2)
            pe.wait_ge(oT_read, H + 2)
            with pe.Fori(0, 2) as c:
                for kq in range(4):
                    tile_full(pe, t, kq, c)
                    for b in range(NB):
                        if kq == 0:
                            pe.wait_ge(vg_done, NB * c + b + 1)
                        for kk in range(4):
                            k = 4 * kq + kk
                            mm = pe.matmul(t.ps[:, b, :], h[:, k, b * P:(b + 1) * P],
                                           t.ring[:, kq, kk * COL:(kk + 1) * COL],
                                           start=(k == 0), stop=(k == KD - 1))
                        if kq == 3 and b < NB - 1:
                            mm.then_inc(vg_bank, 1)
                    mm.then_inc(t.tile_done, 1)
            t.tiles += 8
            pe.sem_inc(mix_ps, 2)
            pe.wait_ge(vg_done, 3 * NB)
            pe.wait_ge(gm_in, 48)
            with pe.Fori(0, 2) as i:
                for j in range(4):
                    n = 4 * i + j
                    pe.wait_ge(z_read, H + n + 1)
                    tile_full(pe, t, j, i)
                    project(pe, t, j % 2, t.ring[:, j, :], h).then_inc(t.tile_done, 1)
                    pe.wait_ge(mix_read, n + 1)
                    pe.wait_ge(v_staged, n + 1)
                    q = 4 + 2 * (j % 2)
                    for b in range(NB):
                        out = t.ps[:, q, (b - 1) * P:b * P] if b else t.ps[:, q + 1, 0:P]
                        pe.matmul(out, staged[j % 2][:, b], ws[:, n, :], start=True, stop=False)
                        mm = pe.matmul(out, t.ones[0:1, :], bs[:, n, :], start=False, stop=True)
                    mm.then_inc(mix_ps, 1)
            t.tiles -= H + 8

        @block.vector
        def _(dve):
            for b in range(NB):
                if b:
                    dve.wait_ge(o_step, 2 * b)
                nc.vector.tensor_tensor(sq, t.d[:, b * HD:(b + 1) * HD], t.d[:, b * HD:(b + 1) * HD],
                                        ALU.mult).then_inc(o_step, 1)
                dve.wait_ge(o_step, 2 * b + 1)
                nc.vector.tensor_reduce(so[:, b, :], sq.rearrange("p (h n) -> p h n", h=H), AX_X,
                                        ALU.add).then_inc(o_step, 1)
            dve.wait_ge(o_step, 2 * NB)
            nc.vector.tensor_scalar(so, so, 1.0 / P, EPS, ALU.mult, ALU.add).then_inc(o_step, 1)
            dve.wait_ge(o_root, 1)
            nc.vector.reciprocal(so, so).then_inc(o_step, 1)
            dve.sem_inc(oT_read, 2)
            dve.sem_inc(mix_read, 2)
            with dve.Fori(0, H // 2) as i:
                for j in range(2):
                    n, q = 2 * i + j, 4 + 2 * j
                    dve.wait_ge(z_read, n + 3)
                    dve.wait_ge(oT_ps, n + 3)
                    nc.vector.scalar_tensor_tensor(out=on[:, n, P:NT], in0=t.ps[:, q, :], scalar=t.dn_norm,
                                                   in1=act_out[j][:, P:NT], op0=ALU.mult, op1=ALU.mult)
                    nc.vector.scalar_tensor_tensor(out=on[:, n, 0:P], in0=t.ps[:, q + 1, 0:P], scalar=t.dn_norm,
                                                   in1=act_out[j][:, 0:P], op0=ALU.mult,
                                                   op1=ALU.mult).then_inc(oT_read, 1)
            dve.wait_ge(vg_done, 3 * NB)
            for b in range(NB):
                if b:
                    dve.wait_ge(vg_step, b)
                nc.vector.tensor_tensor_reduce(sq, vg[:, b, :], vg[:, b, :], 1.0, 0.0, ALU.mult, ALU.add,
                                               sv[:, b:b + 1]).then_inc(vg_step, 1)
            dve.wait_ge(vg_step, NB)
            nc.vector.tensor_scalar(sv, sv, 1.0 / HD, EPS, ALU.mult, ALU.add).then_inc(vg_step, 1)
            dve.wait_ge(o_root, 2)
            nc.vector.reciprocal(sv, sv).then_inc(vg_step, 1)
            dve.wait_ge(vg_step, NB + 2)
            dve.wait_ge(gm_in, 48)
            for b in range(NB):
                nc.vector.scalar_tensor_tensor(out=vg[:, b, :], in0=vg[:, b, :], scalar=sv[:, b:b + 1], in1=gm_norm,
                                               op0=ALU.mult, op1=ALU.mult).then_inc(vg_step, 1)
            with dve.Fori(0, H // 2) as i:
                for j in range(2):
                    n, q = 2 * i + j, 4 + 2 * j
                    dve.wait_ge(z_read, H + n + 3)
                    dve.wait_ge(mix_ps, n + 3)
                    nc.vector.tensor_tensor(gm[:, n, P:NT], t.ps[:, q, :], act_out[j][:, P:NT], ALU.mult)
                    nc.vector.tensor_tensor(gm[:, n, 0:P], t.ps[:, q + 1, 0:P], act_out[j][:, 0:P],
                                            ALU.mult).then_inc(mix_read, 1)

        @block.scalar
        def _(act):
            def both(j, fn):
                nc.scalar.activation(act_out[j][:, P:NT], t.ps[:, 2 * j, :], fn)
                nc.scalar.activation(act_out[j][:, 0:P], t.ps[:, 2 * j + 1, 0:P], fn).then_inc(z_read, 1)

            act.sem_inc(z_read, 2)
            act.sem_inc(vg_done, NB)
            act.wait_ge(o_step, 2 * NB + 1)
            nc.scalar.activation(so, so, ACT.Sqrt).then_inc(o_root, 1)
            with act.Fori(0, H // 2) as i:
                for j in range(2):
                    act.wait_ge(t.tile_done, done_count(t, 2 * i + j))
                    act.wait_ge(oT_read, 2 * i + j + 1)
                    both(j, ACT.Silu)
            t.tiles += H
            with act.Fori(0, 2) as c:
                for b in range(NB):
                    if b < NB - 1:
                        act.wait_ge(vg_bank, (NB - 1) * c + b + 1)
                    else:
                        act.wait_ge(t.tile_done, done_count(t, 4 * c + 3))
                    nc.scalar.activation(vg[:, b, bass.ds(c * COL, COL)], t.ps[:, b, :],
                                         ACT.Gelu_apprx_tanh).then_inc(vg_done, 1)
            act.wait_ge(vg_step, NB + 1)
            nc.scalar.activation(sv, sv, ACT.Sqrt).then_inc(o_root, 1)
            t.tiles += 8
            act.wait_ge(oT_read, H + 2)
            with act.Fori(0, H // 2) as i:
                for j in range(2):
                    act.wait_ge(t.tile_done, done_count(t, 2 * i + j))
                    act.wait_ge(mix_read, 2 * i + j + 1)
                    both(j, ACT.Gelu_apprx_tanh)
            t.tiles -= H + 8
    t.tiles += 2 * H + 8



def merge(nc, t, a):
    h = t.hx[:].rearrange("p (k n) -> p k n", k=KD)
    on = t.c[:, 0:H * NT].rearrange("p (h n) -> p h n", h=H)
    gm = t.c[:, 2 * H * NT:3 * H * NT].rearrange("p (h n) -> p h n", h=H)
    merged = t.d[:, 0:KD * NT].rearrange("p (k n) -> p k n", k=KD)
    sig = [t.d[:, KD * NT + i * NT:KD * NT + (i + 1) * NT] for i in range(2)]
    other = t.d[:, KD * NT + 2 * NT:KD * NT + 3 * NT]
    w_slot = [t.e[:, i * TILE:(i + 1) * TILE] for i in range(2)]
    mod_sum = t.c[:, H * NT:H * NT + 2 * COL].rearrange("p (c n) -> p c n", c=2)
    mod_row, mod_bias = (t.c[0:2, H * NT + i * COL:H * NT + (i + 1) * COL] for i in (2, 3))
    one_of = t.c[:, H * NT + 4 * COL:H * NT + 4 * COL + 4].rearrange("p (c m) -> p c m", c=2)
    first_group = 2 * D // COL
    gate_done, part_done, part_step = t.sem("mg_gate_done"), t.sem("mg_part_done"), t.sem("mg_part_step")
    w_full = [t.sem(f"mg_w_full{i}") for i in range(2)]
    bias_in, mod_step, mod_ps, row_done, row_out, one_done = (t.sem("mg_" + n) for n in (
        "bias_in", "mod_step", "mod_psum", "row_done", "row_out", "one_done"))

    def parts(pair, out):
        return ((t.ps[:, 2 * pair, :], out[:, P:NT]), (t.ps[:, 2 * pair + 1, 0:P], out[:, 0:P]))

    with nc.Block() as block:
        @block.sync
        def _(sp):
            with sp.Fori(1, KD) as n:
                for s, name in enumerate(("w_ga", "w_a", "w_gb", "w_b")):
                    load_tile(sp, t, a[name], 4 * n + s, s, n)
            prefetch(sp, t, 4 * KD, [(a["w_out"], i) for i in range(RING)])

        @block.gpsimd
        def _(pool):
            def row(n):
                pool.wait_ge(row_done, n + 2)
                pool.dma_start(t.mod_rows[:, bass.ds((n + first_group) * COL, COL)], mod_row).then_inc(row_out, 16)

            def load(n, q):
                pool.wait_ge(mod_step, 32 * n + 8 * (q + 1))
                pool.dma_start(w_slot[q % 2], a["w_mod"][bass.ds((n + first_group) * 4 + q, 1)]
                               .rearrange("a p n -> (a p) n")).then_inc(w_full[q % 2], 16)

            def group(n, first=False):
                load(n, 0)
                load(n, 1)
                if not first:
                    row(n - 1)
                pool.dma_start(mod_bias, a["b_mod"][:, bass.ds((n + first_group) * COL, COL)]
                               .partition_broadcast(2)).then_inc(bias_in, 16)
                load(n, 2)
                load(n, 3)

            group(0, True)
            with pool.Fori(1, KD) as n:
                group(n)
            row(KD - 1)
            pool.wait_ge(row_out, 16 * KD)

        @block.tensor
        def _(pe):
            def partition_sum(n):
                pe.wait_ge(mod_step, 32 * n + 48)
                for c in range(2):
                    mm = pe.matmul(t.ps[0:2, 0, :], one_of[:, c, :], mod_sum[:, c, :], start=(c == 0), stop=(c == 1))
                mm.then_inc(mod_ps, 1)

            def channels(n, first=False):
                for s, (x, chunks) in enumerate(((h, KD), (on, H), (h, KD), (gm, H))):
                    pe.wait_ge(gate_done if s % 2 == 0 else part_done, 2 * n + s // 2 + 1)
                    if s == 0 and not first:
                        pe.wait_ge(row_done, n)
                    tile_full(pe, t, s, n)
                    project(pe, t, s, t.ring[:, s, :], x, chunks).then_inc(t.tile_done, 1)
                    if s == 1 and not first:
                        pe.wait_ge(gate_done, 2 * n + 3)
                        partition_sum(n - 1)

            pe.wait_ge(one_done, 3)
            channels(0, True)
            with pe.Fori(1, KD) as n:
                channels(n)
            pe.wait_ge(row_done, KD)
            partition_sum(KD - 1)

        @block.scalar
        def _(act):
            act.sem_inc(gate_done, 2)
            with act.Fori(0, KD) as n:
                for u in range(2):
                    act.wait_ge(t.tile_done, done_count(t, 4 * n + 2 * u))
                    act.wait_ge(part_done, 2 * n + u + 1)
                    (x, o), (xc, oc) = parts(2 * u, sig[u])
                    nc.scalar.activation(o, x, ACT.Sigmoid)
                    nc.scalar.activation(oc, xc, ACT.Sigmoid).then_inc(gate_done, 1)

        @block.vector
        def _(dve):
            dve.sem_inc(part_done, 2)
            dve.sem_inc(part_step, 1)
            dve.sem_inc(mod_step, 16)
            dve.sem_inc(row_done, 1)
            nc.vector.memset(one_of, 0.0).then_inc(one_done, 1)
            dve.wait_ge(one_done, 1)
            for c in range(2):
                nc.vector.memset(one_of[:, c, c:c + 1], 1.0).then_inc(one_done, 1)

            def mod_tile(n, q):
                dve.wait_ge(w_full[q % 2], 32 * n + 16 * (q // 2 + 1))
                for kk in range(4):
                    for c in range(2):
                        w, x = w_slot[q % 2][:, kk * COL:(kk + 1) * COL], t.scond[:, 4 * q + kk, c:c + 1]
                        if q or kk:
                            dve.wait_ge(mod_step, 32 * n + 8 * q + 2 * kk + c + 15)
                            ins = nc.vector.scalar_tensor_tensor(out=mod_sum[:, c, :], in0=w, scalar=x,
                                                                 in1=mod_sum[:, c, :], op0=ALU.mult, op1=ALU.add)
                        else:
                            ins = nc.vector.tensor_scalar(mod_sum[:, c, :], w, x, None, ALU.mult)
                        ins.then_inc(mod_step, 1)

            def finish_group(n, first=False):
                dve.wait_ge(mod_ps, n + 1)
                dve.wait_ge(bias_in, 16 * n + 16)
                if not first:
                    dve.wait_ge(row_out, 16 * n)
                nc.vector.tensor_tensor(mod_row, t.ps[0:2, 0, :], mod_bias, ALU.add).then_inc(row_done, 1)

            def channels(n, first=False, second=False):
                for u, dst in ((0, merged[:, n]), (1, other)):
                    dve.wait_ge(t.tile_done, done_count(t, 4 * n + 2 * u + 1))
                    dve.wait_ge(gate_done, 2 * n + u + 3)
                    if u:
                        dve.wait_ge(part_step, n + 1)
                    for (x, g), o in zip(parts(2 * u + 1, sig[u]), (dst[:, P:NT], dst[:, 0:P])):
                        ins = nc.vector.tensor_tensor(o, x, g, ALU.mult)
                    ins.then_inc(part_done, 1)
                    if not u and not first:
                        finish_group(n - 1, second)
                    if u:
                        dve.wait_ge(part_done, 2 * n + 4)
                        nc.vector.tensor_tensor(merged[:, n], merged[:, n], other, ALU.add).then_inc(part_step, 1)
                    mod_tile(n, 2 * u)
                    mod_tile(n, 2 * u + 1)

            channels(0, first=True)
            channels(1, second=True)
            with dve.Fori(2, KD) as n:
                channels(n)
            finish_group(KD - 1)
            dve.wait_ge(part_step, KD + 1)
    t.tiles += 4 * KD



def output_projection(nc, t, a):
    merged = t.d[:, 0:KD * NT].rearrange("p (k n) -> p k n", k=KD)
    x = t.hx[:].rearrange("p (b n) -> p b n", b=NB)
    gt = t.c[:, 0:2 * D].rearrange("p (c n) -> p c n", c=2)
    pos = t.c[:, 2 * D:6 * D].rearrange("p (b n) -> p b n", b=NB - 1)
    part = t.c[:, 6 * D:6 * D + NB * COL].rearrange("p (b n) -> p b n", b=NB)
    norm, scale_lat, shift_lat = t.e[:, 0:D], t.e[:, D:2 * D], t.d[:, 5 * D:6 * D]
    scale_ctx = t.c[:, 5 * D:6 * D]
    x2_in, gt_in, norm_in, ctx_in = (t.sem("op_" + n) for n in ("x_in", "gt_in", "norm_in", "ctx_in"))
    pos_added, bank_done, part_done, part_added = (t.sem("op_" + n) for n in (
        "pos_added", "bank_done", "part_done", "part_added"))
    row = lambda m, c: t.mod_rows[c:c + 1, m * D:(m + 1) * D].partition_broadcast(P)

    with nc.Block() as block:
        @block.sync
        def _(sp):
            stream(sp, t, a["w_out"], KD, first=1)
            prefetch(sp, t, KD, [(a["w_query"], i) for i in range(RING)])

        @block.scalar
        def _(act):
            for b in range(NB):
                act.dma_start(x[:, b], a["x"][b]).then_inc(x2_in, 16)
            for b in range(NB - 1):
                act.dma_start(pos[:, b], a["c_pos"][b]).then_inc(x2_in, 16)
            for c in range(2):
                act.dma_start(gt[:, c], row(GT1, c)).then_inc(gt_in, 16)
            act.dma_start(norm, a["norm_ffn"].partition_broadcast(P)).then_inc(norm_in, 16)
            act.dma_start(scale_lat, row(SC2, 1)).then_inc(norm_in, 16)
            act.dma_start(shift_lat, row(SH2, 1)).then_inc(norm_in, 16)
            act.wait_ge(pos_added, NB - 1)
            act.dma_start(scale_ctx, row(SC2, 0)).then_inc(ctx_in, 16)

        @block.tensor
        def _(pe):
            with pe.Fori(0, 4) as c:
                for kq in range(4):
                    tile_full(pe, t, kq, c)
                    for b in range(NB):
                        if kq == 0:
                            pe.wait_ge(part_done, NB * c + b + 1)
                        for kk in range(4):
                            k = 4 * kq + kk
                            mm = pe.matmul(t.ps[:, b, :], merged[:, k, b * P:(b + 1) * P],
                                           t.ring[:, kq, kk * COL:(kk + 1) * COL],
                                           start=(k == 0), stop=(k == KD - 1))
                        if kq == 3 and b < NB - 1:
                            mm.then_inc(bank_done, 1)
                    mm.then_inc(t.tile_done, 1)

        @block.vector
        def _(dve):
            dve.sem_inc(part_done, NB)
            dve.wait_ge(x2_in, 16 * (2 * NB - 1))
            for b in range(NB - 1):
                nc.vector.tensor_tensor(x[:, b + 1], x[:, b + 1], pos[:, b], ALU.add).then_inc(pos_added, 1)
            dve.wait_ge(norm_in, 48)
            nc.vector.scalar_tensor_tensor(out=scale_lat, in0=scale_lat, scalar=1.0, in1=norm, op0=ALU.add,
                                           op1=ALU.mult)
            dve.wait_ge(ctx_in, 16)
            nc.vector.scalar_tensor_tensor(out=scale_ctx, in0=scale_ctx, scalar=1.0, in1=norm, op0=ALU.add,
                                           op1=ALU.mult)
            dve.wait_ge(gt_in, 32)
            with dve.Fori(0, 4) as c:
                for b in range(NB):
                    if b < NB - 1:
                        dve.wait_ge(bank_done, (NB - 1) * c + b + 1)
                    else:
                        dve.wait_ge(t.tile_done, done_count(t, 4 * c + 3))
                    dve.wait_ge(part_added, NB * c + b + 1)
                    nc.vector.tensor_tensor(part[:, b], t.ps[:, b, :], gt[:, min(b, 1), bass.ds(c * COL, COL)],
                                            ALU.mult).then_inc(part_done, 1)

        @block.gpsimd
        def _(pool):
            pool.sem_inc(part_added, NB)
            with pool.Fori(0, 4) as c:
                for b in range(NB):
                    pool.wait_ge(part_done, NB * c + b + 1 + NB)
                    cols = x[:, b, bass.ds(c * COL, COL)]
                    nc.gpsimd.tensor_tensor(cols, cols, part[:, b], ALU.add).then_inc(part_added, 1)
    t.tiles += KD



def expert_input(nc, t, a):
    x = t.hx[:].rearrange("p (b n) -> p b n", b=NB)
    h2 = t.c[:, 0:NB * D].rearrange("p (b n) -> p b n", b=NB)
    h2t = t.d[:, 0:KD * NT].rearrange("p (k n) -> p k n", k=KD)
    scale = (t.c[:, 5 * D:6 * D], t.e[:, D:2 * D])
    shift = (t.c[:, 6 * D:7 * D], t.d[:, 5 * D:6 * D])
    ss = t.stat[:, 0:NB]
    ctx_in, sq_done, rstd, scaled, h2_done, turned, copied = (t.sem("ei_" + n) for n in (
        "ctx_in", "sq_done", "rstd", "scaled", "h2_done", "turned", "copied"))
    order = [1, 2, 3, 4, 0]
    with nc.Block() as block:
        @block.sync
        def _(sp):
            sp.dma_start(shift[0], t.mod_rows[0:1, SH2 * D:(SH2 + 1) * D].partition_broadcast(P)).then_inc(ctx_in, 16)

        @block.scalar
        def _(act):
            for b in range(NB):
                nc.scalar.activation(h2[:, b], x[:, b], ACT.Square, accum_out=ss[:, b:b + 1]).then_inc(sq_done, 1)
            act.wait_ge(rstd, 1)
            nc.scalar.activation(ss, ss, ACT.Sqrt).then_inc(rstd, 1)
            for m, b in enumerate(order):
                q = 4 * (m % 2)
                for k in range(4):
                    act.wait_ge(turned, 4 * m + k + 1)
                    nc.scalar.activation(h2t[:, 4 * k:4 * k + 4, b * P:(b + 1) * P],
                                         t.ps[:, q + k, :].rearrange("p (k n) -> p k n", k=4),
                                         ACT.Copy).then_inc(copied, 1)

        @block.vector
        def _(dve):
            dve.wait_ge(sq_done, NB)
            nc.vector.tensor_scalar(ss, ss, 1.0 / D, EPS, ALU.mult, ALU.add).then_inc(rstd, 1)
            dve.wait_ge(rstd, 2)
            nc.vector.reciprocal(ss, ss).then_inc(rstd, 1)
            dve.wait_ge(rstd, 3)
            for b in order:
                nc.vector.scalar_tensor_tensor(out=h2[:, b], in0=x[:, b], scalar=ss[:, b:b + 1],
                                               in1=scale[min(b, 1)], op0=ALU.mult, op1=ALU.mult).then_inc(scaled, 1)

        @block.gpsimd
        def _(pool):
            for m, b in enumerate(order):
                pool.wait_ge(scaled, m + 1)
                if b == 0:
                    pool.wait_ge(ctx_in, 16)
                nc.gpsimd.tensor_tensor(h2[:, b], h2[:, b], shift[min(b, 1)], ALU.add).then_inc(h2_done, 1)

        @block.tensor
        def _(pe):
            for m, b in enumerate(order):
                pe.wait_ge(h2_done, m + 1)
                for k in range(KD):
                    if k % 4 == 0 and m >= 2:
                        pe.wait_ge(copied, 4 * (m - 2) + k // 4 + 1)
                    mm = pe.transpose(t.ps[:, 4 * (m % 2) + k // 4, (k % 4) * P:(k % 4 + 1) * P],
                                      h2[:, b, k * P:(k + 1) * P], t.ident[:])
                    if k % 4 == 3:
                        mm.then_inc(turned, 1)


def routing_views(t):
    n = NB * 2 * H * TOPK
    values = t.d[:, 10240:10240 + n]
    keys = t.d[:, 10240 + n:10240 + n + n // 2].bitcast(mybir.dt.bfloat16)
    return values, keys


def settled(e, t):
    e.sem_inc(t.passed, 1)


def scores(nc, t, a):
    h2t = t.d[:, 0:KD * NT].rearrange("p (k n) -> p k n", k=KD)
    sub_keys = t.e[:, 0:D].rearrange("p (m n) -> p m n", m=2 * H)
    query = [t.e[:, D + i * NT:D + (i + 1) * NT] for i in range(2)]
    rest = t.e[:, D + 2 * NT:D + 3 * NT].rearrange("p (b n) -> p b n", b=NB)
    best = t.c[:, 14336:14336 + NB * TOPK].rearrange("p (b n) -> p b n", b=NB)
    where = t.c[:, 14416:14416 + NB * TOPK].bitcast(U32).rearrange("p (b n) -> p b n", b=NB)
    values, keys = routing_views(t)
    by_half = lambda ap: ap.rearrange("p (b m n) -> p b m n", b=NB, m=2 * H)
    keys_in, query_done, score_ps, score_read, top_step, top_done = (t.sem("sc_" + n) for n in (
        "keys_in", "query_done", "score_ps", "score_read", "top_step", "top_done"))
    tiles = 2 * H
    with nc.Block() as block:
        @block.sync
        def _(sp):
            sp.dma_start(t.e[:, 0:D], a["sub_keys"]).then_inc(keys_in, 16)
            stream(sp, t, a["w_query"], tiles, first=1)

        @block.tensor
        def _(pe):
            def score(n, j):
                pe.wait_ge(query_done, n + 3)
                pe.wait_ge(score_read, n + 1)
                q = 4 + 2 * j
                for b in range(NB):
                    out = t.ps[:, q, (b - 1) * P:b * P] if b else t.ps[:, q + 1, 0:P]
                    mm = pe.matmul(out, query[j][:, b * P:(b + 1) * P], sub_keys[:, n, :], start=True, stop=True)
                mm.then_inc(score_ps, 1)

            def four(i, scored):
                for j in range(4):
                    n = 4 * i + j
                    pe.wait_ge(query_done, n + 1)
                    tile_full(pe, t, j, i)
                    project(pe, t, j % 2, t.ring[:, j, :], h2t).then_inc(t.tile_done, 1)
                    if j in scored:
                        score(n - 1, (j + 1) % 2)

            pe.wait_ge(keys_in, 16)
            four(0, (1, 2, 3))
            with pe.Fori(1, tiles // 4) as i:
                four(i, (0, 1, 2, 3))
            score(tiles - 1, 1)

        @block.scalar
        def _(act):
            act.sem_inc(query_done, 2)
            with act.Fori(0, tiles // 2) as i:
                for j in range(2):
                    n = 2 * i + j
                    act.wait_ge(t.tile_done, done_count(t, n))
                    act.wait_ge(score_read, n + 1)
                    nc.scalar.activation(query[j][:, P:NT], t.ps[:, 2 * j, :], ACT.Copy)
                    nc.scalar.activation(query[j][:, 0:P], t.ps[:, 2 * j + 1, 0:P], ACT.Copy).then_inc(query_done, 1)

        @block.vector
        def _(dve):
            dve.sem_inc(score_read, 2)
            step = Chain(dve, top_step)
            with dve.Fori(0, tiles // 2) as i:
                step.enter(i, 10)
                for j in range(2):
                    n, q = 2 * i + j, 4 + 2 * j
                    row = [t.ps[:, q, (b - 1) * P:b * P] if b else t.ps[:, q + 1, 0:P] for b in range(NB)]
                    dve.wait_ge(score_ps, n + 1)
                    settled(dve, t)
                    for b in range(NB):
                        ins = nc.vector.max(best[:, b, 0:8], row[b])
                    step.step(ins)
                    settled(dve, t)
                    for b in range(NB):
                        nc.vector.max_index(where[:, b, 0:8], best[:, b, 0:8], row[b])
                    for b in range(NB):
                        ins = nc.vector.match_replace(out=rest[:, b], in_to_replace=best[:, b, 0:8],
                                                      in_values=row[b], imm_value=LOWEST)
                    step.step(ins)
                    dve.sem_inc(score_read, 1)
                    settled(dve, t)
                    for b in range(NB):
                        ins = nc.vector.max(best[:, b, 8:16], rest[:, b])
                    step.step(ins)
                    settled(dve, t)
                    for b in range(NB):
                        ins = nc.vector.max_index(where[:, b, 8:16], best[:, b, 8:16], rest[:, b])
                    step.step(ins)
                    nc.vector.tensor_copy(by_half(values)[:, :, n, :], best)
                    step.step(nc.vector.tensor_copy(by_half(keys)[:, :, n, :], where))
                step.leave(tiles // 2)
    t.tiles += tiles



def experts(nc, t, a):
    x = t.hx[:].rearrange("p (b n) -> p b n", b=NB)
    h2 = t.c[:, 0:NB * D].rearrange("p (b n) -> p b n", b=NB)
    diag = t.c[:, 5 * D:6 * D].rearrange("p (e n) -> p e n", e=TOPK)
    total = t.c[:, 6 * D:7 * D]
    u_rows = [t.ring[:, s, :] for s in range(4)]
    v_rows = [t.e[:, 0:D], t.e[:, D:2 * D], t.d[:, 0:D], t.d[:, D:2 * D]]
    gt, norm, h2_block = (t.d[:, i * D:(i + 1) * D] for i in (2, 3, 4))
    values, keys = (ap.rearrange("p (i u n) -> p i u n", u=2, n=TOPK) for ap in routing_views(t))
    w = t.c[:, 7 * D:7 * D + 1024]
    sums = w[:, 0:256].rearrange("p (i j) -> p i j", i=TOPK)
    rest = w[:, 256:512]
    onehot = w[:, 512:1024].rearrange("p (u k j) -> p u k j", u=2, k=TOPK)
    sm = t.cw[:].rearrange("p a b -> p (a b)")
    best, key_pair, expd = sm[:, 0:16], sm[:, 16:48].rearrange("p (u n) -> p u n", u=2), sm[:, 48:64]
    place_f = t.cond[:].rearrange("p k c -> p (k c)").rearrange("p (u n) -> p u n", u=2)
    gate = t.scond[:].rearrange("p k c -> p (k c)").rearrange("p (j n) -> p j n", j=2)
    dots = t.scale1[:].rearrange("p k c -> p (k c)").rearrange("p (j n) -> p j n", j=2)
    weight = t.shift1[:].rearrange("p k c -> p (k c)").rearrange("p (j n) -> p j n", j=2)
    low, total_exp, inv_exp, ss, inv = (t.stat[:, i:i + 1] for i in range(5))
    place = t.place
    s = {n: t.sem("ex_" + n) for n in (
        "norm_in", "gt_in", "routed", "index_kept", "route_step", "exp_done", "u_used", "gate_step", "weight_step", "zeroed", "gelu_done", "weighted",
        "v_used", "added", "h2_staged", "fin_step", "fin_act", "y_done", "y_out")}
    u_full, v_full = [t.sem(f"u_full{i}") for i in range(4)], [t.sem(f"v_full{i}") for i in range(4)]
    row = lambda c: t.mod_rows[c:c + 1, GT2 * D:(GT2 + 1) * D].partition_broadcast(P)

    def each_head(engine, head, stage=None, finish=None):
        def block(b, last):
            with engine.Fori(0, H // 2 - 1) as hp:
                for j in range(2):
                    head(j, b * H + hp * 2 + j, 2, b)
            head(0, b * H + H - 2, 1 if last else 2, b)
            if stage and not last:
                stage(b + 1)
            head(1, b * H + H - 1, 0 if last else 2, b + 1)
            if finish:
                finish(b)
        with engine.Fori(0, NB - 1) as b:
            block(b, False)
        block(NB - 1, True)

    with nc.Block() as block:
        @block.sync
        def _(sp):
            sp.dma_start(norm, a["norm_final"].partition_broadcast(P)).then_inc(s["norm_in"], 16)
            sp.dma_start(gt, row(0)).then_inc(s["gt_in"], 16)
            with sp.Fori(0, NB - 1) as b:
                sp.wait_ge(s["y_done"], b + 1)
                sp.dma_start(gt, row(1)).then_inc(s["gt_in"], 16)
                sp.dma_start(a["y"][bass.ds(b * P, P), :], x[:, b, :]).then_inc(s["y_out"], 16)
            sp.wait_ge(s["y_done"], NB)
            sp.dma_start(a["y"][(NB - 1) * P:, :], x[:, NB - 1, :]).then_inc(s["y_out"], 16)
            sp.wait_ge(s["y_out"], 16 * NB)

        @block.gpsimd
        def _(pool):
            def gather(table, index, rows, full, used, i, e):
                pool.wait_ge(used, i * TOPK + e + 1)
                settled(pool, t)
                nc.gpsimd.indirect_dma_start(
                    rows[e % 4], None, a[table],
                    bass.IndirectOffsetOnAxis(ap=index[:, e:e + 1], axis=0)).then_inc(full[e % 4], 16)

            def u_row(i, j, e):
                gather("peer_u", t.index[:, j, :], u_rows, u_full, s["u_used"], i, e)

            def head(j, i, later, nb):
                pool.wait_ge(s["index_kept"], i + 1)
                if later:
                    pool.wait_ge(s["routed"], i + 2)
                for e in range(TOPK):
                    gather("peer_v", t.index_v[:, j, :], v_rows, v_full, s["v_used"], i, e)
                    if later:
                        u_row(i + 1, 1 - j, e)

            pool.wait_ge(s["routed"], 1)
            for e in range(TOPK):
                u_row(0, 0, e)
            each_head(pool, head)

        @block.tensor
        def _(pe):
            pe.sem_inc(s["v_used"], 4)

            def head(j, i, later, nb):
                pe.wait_ge(s["weighted"], i + 1)
                pe.wait_ge(s["added"], i + 1)
                for e in range(TOPK):
                    pe.wait_ge(v_full[e % 4], 64 * i + 16 * (e // 4 + 1))
                    for c in range(4):
                        mm = pe.matmul(t.ps[:, 4 * j + c, :], diag[:, e, :], v_rows[e % 4][:, c * COL:(c + 1) * COL],
                                       start=(e == 0), stop=(e == TOPK - 1))
                    mm.then_inc(s["v_used"], 1)
            each_head(pe, head)

        @block.scalar
        def _(act):
            def stage(b):
                act.wait_ge(s["u_used"], b * H * TOPK + 4)
                nc.scalar.activation(h2_block, h2[:, b, :], ACT.Copy).then_inc(s["h2_staged"], 1)

            def softmax_exp(i):
                act.wait_ge(s["route_step"], 10 * i + 6)
                nc.scalar.activation(expd, best, ACT.Exp, bias=low, accum_out=total_exp).then_inc(s["exp_done"], 1)

            def gelu(j, i):
                act.wait_ge(s["u_used"], (i + 1) * TOPK + 4)
                nc.scalar.activation(weight[:, j], dots[:, j], ACT.Gelu_apprx_tanh).then_inc(s["gelu_done"], 1)

            def head(j, i, later, nb):
                if later == 2:
                    softmax_exp(i + 2)
                if later:
                    gelu(1 - j, i + 1)

            def finish(b):
                act.wait_ge(s["fin_step"], 4 * b + 2)
                nc.scalar.activation(x[:, b, :], total, ACT.Square, accum_out=ss).then_inc(s["fin_act"], 1)
                act.wait_ge(s["fin_step"], 4 * b + 3)
                nc.scalar.activation(inv, ss, ACT.Sqrt).then_inc(s["fin_act"], 1)

            stage(0)
            softmax_exp(0)
            softmax_exp(1)
            gelu(0, 0)
            each_head(act, head, stage, finish)

        @block.vector
        def _(dve):
            dve.sem_inc(s["u_used"], 4)
            dve.sem_inc(s["added"], 2)
            step = Chain(dve, s["route_step"])

            def keep_index(i, j):
                dve.wait_ge(s["routed"], i + 1)
                nc.vector.tensor_copy(t.index_v[:, j, :], t.index[:, j, :]).then_inc(s["index_kept"], 1)

            def route(i, j):
                step.base, step.count = 10 * i, 0
                gate_step.base, gate_step.count = 2 * i, 0
                step.sig(nc.vector.tensor_tensor(
                    sums, values[:, i, 0, :].unsqueeze(2).to_broadcast([P, TOPK, TOPK]),
                    values[:, i, 1, :].unsqueeze(1).to_broadcast([P, TOPK, TOPK]), ALU.add))
                step.sync()
                flat = w[:, 0:256]
                settled(dve, t)
                step.step(nc.vector.max(best[:, 0:8], flat))
                settled(dve, t)
                nc.vector.max_index(place[:, 0, 0:8], best[:, 0:8], flat)
                step.step(nc.vector.match_replace(out=rest, in_to_replace=best[:, 0:8], in_values=flat,
                                                  imm_value=LOWEST))
                settled(dve, t)
                step.step(nc.vector.max(best[:, 8:16], rest))
                settled(dve, t)
                step.step(nc.vector.max_index(place[:, 0, 8:16], best[:, 8:16], rest))
                nc.vector.tensor_scalar(place[:, 1, :], place[:, 0, :], 4, None, ALU.logical_shift_right)
                nc.vector.tensor_scalar(low, best[:, 0:1], -1.0, None, ALU.mult)
                step.step(nc.vector.tensor_scalar(place[:, 2, :], place[:, 0, :], 15, None, ALU.bitwise_and))
                step.step(nc.vector.tensor_copy(place_f, place[:, 1:3, :]))
                step.step(nc.vector.tensor_tensor(
                    onehot, place_f.unsqueeze(3).to_broadcast([P, 2, TOPK, TOPK]),
                    t.iota.unsqueeze(1).unsqueeze(1).to_broadcast([P, 2, TOPK, TOPK]), ALU.is_equal))
                step.step(nc.vector.tensor_tensor(
                    onehot, onehot, keys[:, i, :, :].unsqueeze(2).to_broadcast([P, 2, TOPK, TOPK]), ALU.mult))
                step.step(nc.vector.tensor_reduce(key_pair, onehot, AX_X, ALU.add))
                nc.vector.scalar_tensor_tensor(out=t.index[:, j, :], in0=key_pair[:, 0], scalar=float(NKEYS),
                                               in1=key_pair[:, 1], op0=ALU.mult, op1=ALU.add).then_inc(s["routed"], 1)
                dve.wait_ge(s["exp_done"], i + 1)
                gate_step.step(nc.vector.reciprocal(inv_exp, total_exp))
                gate_step.step(nc.vector.tensor_scalar(gate[:, j], expd, inv_exp, None, ALU.mult))

            def dot(j, i, e):
                dve.wait_ge(u_full[e % 4], 64 * i + 16 * (e // 4 + 1))
                nc.vector.tensor_tensor_reduce(u_rows[e % 4], u_rows[e % 4], h2_block, 1.0, 0.0, ALU.mult,
                                               ALU.add, dots[:, j, e:e + 1]).then_inc(s["u_used"], 1)

            def weigh(j, i):
                dve.wait_ge(s["gelu_done"], i + 1)
                nc.vector.tensor_tensor(weight[:, j], weight[:, j], gate[:, j], ALU.mult).then_inc(s["weight_step"], 1)
                dve.wait_ge(s["weight_step"], i + 1)
                nc.vector.tensor_tensor(diag, over(t.ident[:], TOPK), wide(weight[:, j], P),
                                        ALU.mult).then_inc(s["weighted"], 1)

            def head(j, i, later, nb):
                if later:
                    dve.wait_ge(s["h2_staged"], nb + 1)
                    for e in range(TOPK):
                        if e == 4:
                            keep_index(i + 1, 1 - j)
                            if later == 2:
                                route(i + 2, j)
                        dot(1 - j, i + 1, e)
                dve.wait_ge(s["v_used"], (i + 1) * TOPK + 4)
                dve.wait_ge(s["added"], i + 2)
                nc.vector.tensor_tensor(total, total, t.ps[:, 4 * j:4 * j + 4, :].rearrange("p c n -> p (c n)"),
                                        ALU.add).then_inc(s["added"], 1)
                if later:
                    weigh(1 - j, i + 1)

            def finish(b):
                dve.wait_ge(s["added"], (b + 1) * H + 2)
                dve.wait_ge(s["gt_in"], 16 * (b + 1))
                nc.vector.tensor_tensor(total, total, gt, ALU.mult).then_inc(s["fin_step"], 1)
                dve.wait_ge(s["fin_step"], 4 * b + 1)
                nc.vector.tensor_tensor(total, total, x[:, b, :], ALU.add).then_inc(s["fin_step"], 1)
                dve.wait_ge(s["fin_act"], 2 * b + 1)
                nc.vector.tensor_scalar(ss, ss, 1.0 / D, EPS, ALU.mult, ALU.add).then_inc(s["fin_step"], 1)
                dve.wait_ge(s["fin_act"], 2 * b + 2)
                nc.vector.reciprocal(inv, inv).then_inc(s["fin_step"], 1)
                dve.wait_ge(s["fin_step"], 4 * b + 4)
                nc.vector.scalar_tensor_tensor(out=x[:, b, :], in0=total, scalar=inv, in1=norm, op0=ALU.mult,
                                               op1=ALU.mult).then_inc(s["y_done"], 1)
                dve.wait_ge(s["y_done"], b + 1)
                nc.vector.memset(total, 0.0).then_inc(s["zeroed"], 1)
                dve.wait_ge(s["zeroed"], b + 2)

            gate_step = Chain(dve, s["gate_step"])
            nc.vector.memset(total, 0.0).then_inc(s["zeroed"], 1)
            route(0, 0)
            keep_index(0, 0)
            route(1, 1)
            dve.wait_ge(s["h2_staged"], 1)
            for e in range(TOPK):
                dot(0, 0, e)
            weigh(0, 0)
            dve.wait_ge(s["zeroed"], 1)
            dve.wait_ge(s["norm_in"], 16)
            each_head(dve, head, finish=finish)


def build(nc, a):
    with ExitStack() as ctx:
        t = allocate(nc, ctx)
        for phase in (modulation, mixer_input, qkv, deltanet, branches, merge, output_projection, expert_input,
                      scores, experts):
            phase(nc, t, a)



def feature_tiles(w):
    k, n = w.shape
    return np.ascontiguousarray(w.reshape(k // P, P, n // P, P).transpose(2, 1, 0, 3)).reshape(n // P, P, k)


def row_tiles(w):
    n = w.shape[1] // COL
    return np.ascontiguousarray(w.reshape(4, 4, P, n, COL).transpose(3, 0, 2, 1, 4)).reshape(4 * n, P, TILE)


def constants():
    i = np.arange(P)
    ident = np.eye(P, dtype=np.float32)
    tri = np.stack([i[:, None] <= i[None, :], i[:, None] >= i[None, :]], 1).astype(np.float32)
    lower = []
    for level in range(LEVELS):
        b = 2 ** level
        half = (i // b) % 2
        lower.append(-((i[:, None] // (2 * b) == i[None, :] // (2 * b)) & (half[:, None] == 1) & (half[None, :] == 0)).astype(np.float32))
    masks = np.stack([np.stack(lower), np.stack([m.T for m in lower])])
    strict = i[:, None] > i[None, :]
    above = np.stack([np.where(strict, 0, BIG), np.where(strict.T, 0, BIG)])
    below = np.stack([np.where(strict.T | (ident > 0), 0, -BIG), np.where(strict | (ident > 0), 0, -BIG)])
    masks = np.concatenate([masks.transpose(2, 0, 1, 3).reshape(P, -1), above.transpose(1, 0, 2).reshape(P, -1),
                            below.transpose(1, 0, 2).reshape(P, -1)], 1).astype(np.float32)
    small = np.concatenate([np.tile(np.arange(16), (P, 1)), np.tile(np.repeat([P ** -0.5, 1.0], H), (P, 1))], 1)
    tokens = np.arange(LAT)
    quarter = D // 4
    freq = (1.0 / (np.float32(10000.0) ** (np.arange(quarter, dtype=np.float32) / np.float32(quarter)))).astype(np.float32)
    def enc(p):
        ang = p.astype(np.float32)[:, None] * freq
        return np.concatenate([np.sin(ang), np.cos(ang)], 1)
    pos = np.concatenate([enc(tokens // 64), enc(tokens % 64)], 1).astype(np.float32)
    return {"c_ident": ident, "c_tri": tri.reshape(P, 2 * P), "c_masks": masks,
            "c_small": small.astype(np.float32), "c_pos": pos.reshape(NB - 1, P, D)}


def lay_out(i):
    w = i["w_in"][0]
    at = np.cumsum([0, 3 * HD, HD, 4 * H, HD, HD, D, D])
    qkv_w, z_w, gates_w, u_w, vg_w, ga_w, gb_w = (w[:, x:y] for x, y in zip(at[:-1], at[1:]))
    cond = np.stack([i["c_ctx"], i["c"][0]])
    row = lambda x: np.ascontiguousarray(x).reshape(1, -1)
    return {
        "x": np.concatenate([i["x_prompt"].reshape(1, P, D), i["x_sample"].reshape(NB - 1, P, D)]),
        "cond": np.ascontiguousarray(cond.reshape(2, KD, P).transpose(2, 1, 0)),
        "w_mod": row_tiles(i["w_mod"][0]), "b_mod": row(i["b_mod"][0]),
        "norm_mix": np.ascontiguousarray(i["norm_mix"][0].reshape(KD, P).T),
        "w_qkv": feature_tiles(qkv_w), "w_z": feature_tiles(z_w), "w_u": feature_tiles(u_w),
        "w_vg": row_tiles(vg_w), "w_ga": feature_tiles(ga_w), "w_gb": feature_tiles(gb_w),
        "w_gates": np.ascontiguousarray(gates_w.reshape(KD, P, 4 * H).transpose(1, 0, 2)).reshape(P, KD * 4 * H),
        "conv_w": np.ascontiguousarray(i["conv_w"][0].reshape(3, 3 * H, P).transpose(2, 1, 0)).reshape(P, 9 * H),
        "a_log": row(i["dn_a_log"][0]), "dt_bias": row(i["dn_dt_bias"][0]),
        "dn_norm": i["dn_norm"][0].reshape(P, 1),
        "state": i["state_delta"][0, 0],
        "gm_norm": row(i["gm_norm"][0]),
        "gm_w_s": np.ascontiguousarray(i["gm_w_s"][0].transpose(2, 0, 1)).reshape(P, HD),
        "gm_b_s": row(i["gm_b_s"][0]),
        "w_a": feature_tiles(i["w_branch_a"][0]), "w_b": feature_tiles(i["w_branch_b"][0]),
        "w_out": row_tiles(i["w_out"][0]), "norm_ffn": row(i["norm_ffn"][0]),
        "w_query": feature_tiles(i["peer_w_query"][0].reshape(D, D)),
        "sub_keys": np.ascontiguousarray(i["peer_sub_keys"][0].reshape(2 * H, NKEYS, P).transpose(2, 0, 1)).reshape(P, 2 * HD),
        "peer_u": i["peer_u"][0], "peer_v": i["peer_v"][0],
        "norm_final": row(i["norm_final"]),
        **constants(),
    }


OUTS = {"y": (NT, D), "new_state": (2, H, P, P)}


def kernel(**inputs):
    import concourse.bacc as bacc
    from concourse.bass_utils import run_bass_kernel_spmd

    arrays = lay_out({k: np.asarray(v) for k, v in inputs.items()})
    nc = bacc.Bacc("TRN2", target_bir_lowering=False, num_devices=1)
    a = {k: nc.dram_tensor(k, v.shape, F32, kind="ExternalInput").ap() for k, v in arrays.items()}
    a |= {k: nc.dram_tensor(k, v, F32, kind="ExternalOutput").ap() for k, v in OUTS.items()}
    build(nc, a)
    got = run_bass_kernel_spmd(nc, [arrays], core_ids=[0]).results[0]
    y = got["y"]
    return (y[0:P].reshape(1, P, D), y[P:].reshape(1, LAT, D), got["new_state"].reshape(1, 1, 2, H, P, P))
```
